# Optimizing a Trainium2 kernel written in Bass

```python
import math
import jax, jax.numpy as jnp
from jax import lax
import numpy as np

D_MODEL = 1024
BATCH = 1
SEQ = 128
DEPTH = 1
DEC_BATCH = 1
DEC_SEQ = 512
PAST_LEN = 128

GRID_W = 64
D_MIX = D_MODEL
N_HEADS_A = 8
HEAD_DIM_A = 64
D_ATT = N_HEADS_A * HEAD_DIM_A
WIN_R = 8
WIN_C = 16
Q_BLOCK = 128
D_RNN = D_MODEL // 4
RG_BLOCKS = 4
RG_BLK = D_RNN // RG_BLOCKS
RG_CONV = 4
RG_C = 8.0
D_HY = D_MODEL // 4
HY_ORDER = 2
HY_CONV = 3
POS_EMB_DIM = 33
FILTER_HIDDEN = 64
N_GROUPS = 4
EXPERTS_PER_GROUP = 4
N_EXPERTS = N_GROUPS * EXPERTS_PER_GROUP
D_EXPERT = 256
TOP_K = 2
D_IN = 3 * D_ATT + 2 * D_RNN + 3 * D_HY
ALPHA = (2.0 * DEPTH) ** 0.25
OUT_SCALE = (8.0 * DEPTH) ** -0.25
LN_EPS = 1e-5
F32 = jnp.float32

kernel_name = 'hybrid_natten_rglru_hyena_hmoe_step'

def layer_norm(x, g=None, b=None):
    xf = x.astype(F32)
    mu = jnp.mean(xf, axis=-1, keepdims=True)
    var = jnp.mean(jnp.square(xf - mu), axis=-1, keepdims=True)
    y = (xf - mu) * lax.rsqrt(var + LN_EPS)
    if g is not None:
        y = y * g.astype(F32) + b.astype(F32)
    return y.astype(x.dtype)

def modulation(cond, w_mod, b_mod):
    m = jnp.einsum('...d,de->...e', jax.nn.silu(cond), w_mod) + b_mod
    return jnp.split(m, 6, axis=-1)

def depthwise_conv(x, w, b, pad_left):
    width = w.shape[0]
    L = x.shape[1]
    xp = jnp.pad(x, ((0, 0), (pad_left, width - 1 - pad_left), (0, 0)))
    y = b
    for k in range(width):
        y = y + xp[:, k:k + L] * w[k]
    return y

def split_projection(u, w_in):
    Bn, L, _ = u.shape
    z = jnp.einsum('bld,de->ble', u, w_in)
    q, k, v, xr, gate, hy = jnp.split(
        z, [D_ATT, 2 * D_ATT, 3 * D_ATT, 3 * D_ATT + D_RNN, 3 * D_ATT + 2 * D_RNN], axis=-1)
    heads = lambda t: t.reshape(Bn, L, N_HEADS_A, HEAD_DIM_A)
    return heads(q), heads(k), heads(v), xr, gate, hy

def context_attention(q, k, v):
    Bn, Lc, H, d = q.shape
    scale = d ** -0.5
    qb = q.reshape(Bn, Lc // Q_BLOCK, Q_BLOCK, H, d).transpose(1, 0, 2, 3, 4)

    def block(qi):
        s = jnp.einsum('bqhd,bkhd->bhqk', qi, k).astype(F32) * scale
        p = jax.nn.softmax(s, axis=-1).astype(v.dtype)
        return jnp.einsum('bhqk,bkhd->bqhd', p, v)

    o = lax.map(block, qb)
    return o.transpose(1, 0, 2, 3, 4).reshape(Bn, Lc, H * d)

def neighbourhood_attention(q, k, v, k_ctx, v_ctx, rpb):
    Bn, L, H, d = q.shape
    rows = L // GRID_W
    wr = min(WIN_R, rows)
    scale = d ** -0.5
    qg = q.reshape(Bn, rows, GRID_W, H, d).transpose(1, 0, 2, 3, 4)
    kg = k.reshape(Bn, rows, GRID_W, H, d)
    vg = v.reshape(Bn, rows, GRID_W, H, d)
    cols = jnp.arange(GRID_W)
    c_start = jnp.clip(cols - WIN_C // 2, 0, GRID_W - WIN_C)
    col_mask = (cols[None, :] >= c_start[:, None]) & (cols[None, :] < c_start[:, None] + WIN_C)
    dc_idx = jnp.clip(cols[None, :] - cols[:, None], -(WIN_C - 1), WIN_C - 1) + (WIN_C - 1)
    rpb_c = rpb[:, :, dc_idx]

    def row(args):
        r, qr = args
        start = jnp.clip(r - wr // 2, 0, rows - wr)
        kb = lax.dynamic_slice_in_dim(kg, start, wr, axis=1)
        vb = lax.dynamic_slice_in_dim(vg, start, wr, axis=1)
        dr_idx = start + jnp.arange(wr) - r + (WIN_R - 1)
        bias = jnp.take(rpb_c, dr_idx, axis=1).transpose(0, 2, 1, 3)
        s_lat = jnp.einsum('bqhd,bikhd->bhqik', qr, kb).astype(F32) * scale + bias.astype(F32)
        s_lat = jnp.where(col_mask[None, None, :, None, :], s_lat, -jnp.inf)
        s_ctx = jnp.einsum('bqhd,bchd->bhqc', qr, k_ctx).astype(F32) * scale
        s = jnp.concatenate([s_lat.reshape(Bn, H, GRID_W, wr * GRID_W), s_ctx], axis=-1)
        p = jax.nn.softmax(s, axis=-1).astype(v.dtype)
        p_lat = p[..., :wr * GRID_W].reshape(Bn, H, GRID_W, wr, GRID_W)
        p_ctx = p[..., wr * GRID_W:]
        return (jnp.einsum('bhqik,bikhd->bqhd', p_lat, vb)
                + jnp.einsum('bhqc,bchd->bqhd', p_ctx, v_ctx))

    o = lax.map(row, (jnp.arange(rows), qg))
    return o.transpose(1, 0, 2, 3, 4).reshape(Bn, L, H * d)

def linear_scan(a, b, h0):
    if h0 is not None:
        b = b.at[:, 0].add(a[:, 0] * h0)

    def combine(e1, e2):
        a1, b1 = e1
        a2, b2 = e2
        return a1 * a2, a2 * b1 + b2

    _, h = lax.associative_scan(combine, (a, b), axis=1)
    return h

def rglru(xr, gate, conv_w, conv_b, wa, ba, wx, bx, lam, h0):
    Bn, L, _ = xr.shape
    xc = depthwise_conv(xr, conv_w, conv_b, RG_CONV // 2)
    xb = xc.reshape(Bn, L, RG_BLOCKS, RG_BLK)
    r = jax.nn.sigmoid(jnp.einsum('blnk,enkj->eblnj', xb, wa).reshape(2, Bn, L, D_RNN)
                       + ba[:, None, None, :])
    i = jax.nn.sigmoid(jnp.einsum('blnk,enkj->eblnj', xb, wx).reshape(2, Bn, L, D_RNN)
                       + bx[:, None, None, :])
    log_a = -RG_C * r.astype(F32) * jax.nn.softplus(-lam.astype(F32))[:, None, None, :]
    a = jnp.exp(log_a)
    b = jnp.sqrt(-jnp.expm1(2.0 * log_a)) * i.astype(F32) * xc.astype(F32)[None]
    h0f = None if h0 is None else h0[:, 0].astype(F32)
    h0b = None if h0 is None else h0[:, 1].astype(F32)
    h_f = linear_scan(a[0], b[0], h0f)
    h_b = jnp.flip(linear_scan(jnp.flip(a[1], axis=1), jnp.flip(b[1], axis=1), h0b), axis=1)
    y = (h_f + h_b).astype(xr.dtype) * jax.nn.gelu(gate)
    return y, h_f, h_b

def hyena_filters(L, w1, b1, w2, b2, w3, freq, decay):
    pos = jnp.arange(L, dtype=F32)
    t = jnp.linspace(0.0, 1.0, L, dtype=F32)
    bands = (POS_EMB_DIM - 1) // 2
    f = jnp.linspace(1e-4, bands - 1, bands, dtype=F32)
    ang = (2.0 * math.pi / L) * pos[:, None] * f[None, :]
    feats = jnp.concatenate([t[:, None], jnp.cos(ang), -jnp.sin(ang)], axis=-1)
    freq = freq.astype(F32)
    h = jnp.sin(freq[0] * (feats @ w1.astype(F32) + b1.astype(F32)))
    h = jnp.sin(freq[1] * (h @ w2.astype(F32) + b2.astype(F32)))
    h = (h @ w3.astype(F32)).reshape(L, 2 * HY_ORDER, D_HY).transpose(1, 0, 2)
    window = jnp.exp(-t[None, :, None] * jnp.abs(decay.astype(F32))[:, None, :])
    return h * window

def hyena(hy, conv_w, conv_b, w1, b1, w2, b2, w3, freq, decay, skip):
    Bn, L, _ = hy.shape
    hc = depthwise_conv(hy, conv_w, conv_b, HY_CONV // 2)
    v, x1, x2 = jnp.split(hc, 3, axis=-1)
    filt = hyena_filters(L, w1, b1, w2, b2, w3, freq, decay)
    f_fwd, f_bwd = filt[:HY_ORDER], filt[HY_ORDER:]
    circ_filter = jnp.concatenate(
        [f_fwd, jnp.zeros((HY_ORDER, 1, D_HY), F32), jnp.flip(f_bwd[:, 1:], axis=1)], axis=1)
    filt_f = jnp.fft.rfft(circ_filter, axis=1)
    z = v.astype(F32)
    for n, g in enumerate((x1, x2)):
        zf = jnp.fft.rfft(z, n=2 * L, axis=1)
        conv = jnp.fft.irfft(zf * filt_f[n][None], n=2 * L, axis=1)[:, :L]
        z = g.astype(F32) * (conv + skip[n].astype(F32) * z)
    return z.astype(hy.dtype)

def hier_moe(u, wg, bg, we, be, w_gate, w_up, w_down):
    Bn, L, _ = u.shape
    g_logits = (jnp.einsum('bld,dg->blg', u, wg) + bg).astype(F32)
    g_idx = jnp.argmax(g_logits, axis=-1)
    p_group = jnp.take_along_axis(jax.nn.softmax(g_logits, axis=-1), g_idx[..., None], axis=-1)
    e_logits = (jnp.einsum('bld,de->ble', u, we) + be).astype(F32)
    e_logits = e_logits.reshape(Bn, L, N_GROUPS, EXPERTS_PER_GROUP)
    e_sel = jnp.take_along_axis(e_logits, g_idx[..., None, None], axis=2)[:, :, 0]
    top_p, top_i = lax.top_k(jax.nn.softmax(e_sel, axis=-1), TOP_K)
    top_p = top_p / jnp.sum(top_p, axis=-1, keepdims=True)
    expert_id = g_idx[..., None] * EXPERTS_PER_GROUP + top_i
    combine = jnp.sum(jax.nn.one_hot(expert_id, N_EXPERTS, dtype=F32)
                      * (p_group * top_p)[..., None], axis=-2).astype(u.dtype)
    h = jax.nn.silu(jnp.einsum('bld,edf->blef', u, w_gate)) * jnp.einsum('bld,edf->blef', u, w_up)
    return jnp.einsum('blef,ble,efd->bld', h, combine, w_down)

def setup_inputs(seed: int = 0) -> dict:
    key = jax.random.key(seed)
    keys = iter(jax.random.split(key, 64))

    def nrm(shape, scale=1.0):
        return jax.random.normal(next(keys), shape, jnp.float32) * scale

    x_prompt = nrm((BATCH, SEQ, D_MODEL))
    x_sample = nrm((DEC_BATCH, DEC_SEQ, D_MODEL))
    cache_k = nrm((DEC_BATCH, DEPTH, PAST_LEN, N_HEADS_A, HEAD_DIM_A))
    cache_v = nrm((DEC_BATCH, DEPTH, PAST_LEN, N_HEADS_A, HEAD_DIM_A))
    state_rglru = nrm((DEC_BATCH, DEPTH, 2, D_RNN), 0.5)
    c = nrm((DEC_BATCH, D_MODEL))
    c_ctx = nrm((D_MODEL,))
    w_mod = nrm((DEPTH, D_MODEL, 6 * D_MODEL), D_MODEL ** -0.5)
    b_mod = nrm((DEPTH, 6 * D_MODEL), 0.02)
    w_in = nrm((DEPTH, D_MODEL, D_IN), D_MODEL ** -0.5)
    attn_rpb = nrm((DEPTH, N_HEADS_A, 2 * WIN_R - 1, 2 * WIN_C - 1), 0.1)
    rg_conv_w = nrm((DEPTH, RG_CONV, D_RNN), RG_CONV ** -0.5)
    rg_conv_b = nrm((DEPTH, D_RNN), 0.01)
    rg_wa = nrm((DEPTH, 2, RG_BLOCKS, RG_BLK, RG_BLK), RG_BLK ** -0.5)
    rg_ba = nrm((DEPTH, 2, D_RNN), 0.01)
    rg_wx = nrm((DEPTH, 2, RG_BLOCKS, RG_BLK, RG_BLK), RG_BLK ** -0.5)
    rg_bx = nrm((DEPTH, 2, D_RNN), 0.01)
    a0 = jax.random.uniform(next(keys), (DEPTH, 2, D_RNN), jnp.float32, 0.9, 0.999)
    p = a0 ** (1.0 / RG_C)
    rg_lambda = jnp.log(p) - jnp.log1p(-p)
    hy_conv_w = nrm((DEPTH, HY_CONV, 3 * D_HY), HY_CONV ** -0.5)
    hy_conv_b = nrm((DEPTH, 3 * D_HY), 0.01)
    hy_w1 = nrm((DEPTH, POS_EMB_DIM, FILTER_HIDDEN), POS_EMB_DIM ** -0.5)
    hy_b1 = nrm((DEPTH, FILTER_HIDDEN), 0.1)
    hy_w2 = nrm((DEPTH, FILTER_HIDDEN, FILTER_HIDDEN), FILTER_HIDDEN ** -0.5)
    hy_b2 = nrm((DEPTH, FILTER_HIDDEN), 0.1)
    hy_w3 = nrm((DEPTH, FILTER_HIDDEN, 2 * HY_ORDER * D_HY), 0.1 * FILTER_HIDDEN ** -0.5)
    hy_freq = 1.0 + nrm((DEPTH, 2, FILTER_HIDDEN), 0.05)
    decay_base = jnp.linspace(math.log(100.0) / 1.5, math.log(100.0) / 0.3, D_HY, dtype=jnp.float32)
    hy_decay = decay_base * (1.0 + nrm((DEPTH, 2 * HY_ORDER, D_HY), 0.05))
    hy_skip = nrm((DEPTH, HY_ORDER, D_HY), 0.5)
    w_out = nrm((DEPTH, D_MIX, D_MODEL), OUT_SCALE * D_MIX ** -0.5)
    ln1_g = 1.0 + nrm((DEPTH, D_MODEL), 0.01)
    ln1_b = nrm((DEPTH, D_MODEL), 0.01)
    router_wg = nrm((DEPTH, D_MODEL, N_GROUPS), D_MODEL ** -0.5)
    router_bg = nrm((DEPTH, N_GROUPS), 0.01)
    router_we = nrm((DEPTH, D_MODEL, N_EXPERTS), D_MODEL ** -0.5)
    router_be = nrm((DEPTH, N_EXPERTS), 0.01)
    moe_w_gate = nrm((DEPTH, N_EXPERTS, D_MODEL, D_EXPERT), D_MODEL ** -0.5)
    moe_w_up = nrm((DEPTH, N_EXPERTS, D_MODEL, D_EXPERT), D_MODEL ** -0.5)
    moe_w_down = nrm((DEPTH, N_EXPERTS, D_EXPERT, D_MODEL), OUT_SCALE * D_EXPERT ** -0.5)
    ln2_g = 1.0 + nrm((DEPTH, D_MODEL), 0.01)
    ln2_b = nrm((DEPTH, D_MODEL), 0.01)
    return {'x_prompt': x_prompt, 'x_sample': x_sample, 'cache_k': cache_k, 'cache_v': cache_v,
            'state_rglru': state_rglru, 'c': c, 'c_ctx': c_ctx, 'w_mod': w_mod, 'b_mod': b_mod,
            'w_in': w_in, 'attn_rpb': attn_rpb, 'rg_conv_w': rg_conv_w, 'rg_conv_b': rg_conv_b,
            'rg_wa': rg_wa, 'rg_ba': rg_ba, 'rg_wx': rg_wx, 'rg_bx': rg_bx, 'rg_lambda': rg_lambda,
            'hy_conv_w': hy_conv_w, 'hy_conv_b': hy_conv_b, 'hy_w1': hy_w1, 'hy_b1': hy_b1,
            'hy_w2': hy_w2, 'hy_b2': hy_b2, 'hy_w3': hy_w3, 'hy_freq': hy_freq, 'hy_decay': hy_decay,
            'hy_skip': hy_skip, 'w_out': w_out, 'ln1_g': ln1_g, 'ln1_b': ln1_b,
            'router_wg': router_wg, 'router_bg': router_bg, 'router_we': router_we,
            'router_be': router_be, 'moe_w_gate': moe_w_gate, 'moe_w_up': moe_w_up,
            'moe_w_down': moe_w_down, 'ln2_g': ln2_g, 'ln2_b': ln2_b}

def reference(x_prompt, x_sample, cache_k, cache_v, state_rglru, c, c_ctx, w_mod, b_mod, w_in,
              attn_rpb, rg_conv_w, rg_conv_b, rg_wa, rg_ba, rg_wx, rg_bx, rg_lambda,
              hy_conv_w, hy_conv_b, hy_w1, hy_b1, hy_w2, hy_b2, hy_w3, hy_freq, hy_decay, hy_skip,
              w_out, ln1_g, ln1_b, router_wg, router_bg, router_we, router_be,
              moe_w_gate, moe_w_up, moe_w_down, ln2_g, ln2_b):
    xp = x_prompt
    xs = x_sample
    new_k, new_v, new_h = [], [], []
    for l in range(DEPTH):
        rg_p = (rg_conv_w[l], rg_conv_b[l], rg_wa[l], rg_ba[l], rg_wx[l], rg_bx[l], rg_lambda[l])
        hy_p = (hy_conv_w[l], hy_conv_b[l], hy_w1[l], hy_b1[l], hy_w2[l], hy_b2[l], hy_w3[l],
                hy_freq[l], hy_decay[l], hy_skip[l])
        moe_p = (router_wg[l], router_bg[l], router_we[l], router_be[l],
                 moe_w_gate[l], moe_w_up[l], moe_w_down[l])

        sh1, sc1, g1, sh2, sc2, g2 = modulation(c_ctx[None, None, :], w_mod[l], b_mod[l])
        u = layer_norm(xp) * (1.0 + sc1) + sh1
        q, k, v, xr, gate, hy = split_projection(u, w_in[l])
        att = context_attention(q, k, v)
        rg, h_f, h_b = rglru(xr, gate, *rg_p, None)
        hyo = hyena(hy, *hy_p)
        mix = jnp.concatenate([att, rg, hyo], axis=-1) @ w_out[l]
        xp = layer_norm(ALPHA * xp + g1 * mix, ln1_g[l], ln1_b[l])
        u = layer_norm(xp) * (1.0 + sc2) + sh2
        xp = layer_norm(ALPHA * xp + g2 * hier_moe(u, *moe_p), ln2_g[l], ln2_b[l])
        new_k.append(k)
        new_v.append(v)
        new_h.append(jnp.stack([h_f[:, -1], h_b[:, 0]], axis=1).astype(x_prompt.dtype))

        sh1, sc1, g1, sh2, sc2, g2 = modulation(c[:, None, :], w_mod[l], b_mod[l])
        u = layer_norm(xs) * (1.0 + sc1) + sh1
        q, k, v, xr, gate, hy = split_projection(u, w_in[l])
        att = neighbourhood_attention(q, k, v, cache_k[:, l], cache_v[:, l], attn_rpb[l])
        rg, _, _ = rglru(xr, gate, *rg_p, state_rglru[:, l])
        hyo = hyena(hy, *hy_p)
        mix = jnp.concatenate([att, rg, hyo], axis=-1) @ w_out[l]
        xs = layer_norm(ALPHA * xs + g1 * mix, ln1_g[l], ln1_b[l])
        u = layer_norm(xs) * (1.0 + sc2) + sh2
        xs = layer_norm(ALPHA * xs + g2 * hier_moe(u, *moe_p), ln2_g[l], ln2_b[l])

    return (xp, xs, jnp.stack(new_k, axis=1), jnp.stack(new_v, axis=1), jnp.stack(new_h, axis=1))


_drawn_inputs = setup_inputs


def setup_inputs(seed=0):
    import zlib

    import numpy as np

    out = dict(_drawn_inputs(seed))
    spreads = {}
    factors = {'cache_k': 3.07,
     'cache_v': 3.077,
     'attn_rpb': 64.0,
     'rg_conv_b': 3.495,
     'rg_ba': 47.526,
     'rg_bx': 8.0,
     'hy_conv_b': 16.206,
     'hy_freq': 3.014,
     'ln1_g': 111.826,
     'ln1_b': 106.355,
     'router_bg': 200.0,
     'router_be': 200.0,
     'ln2_g': 175.753,
     'ln2_b': 170.885,
     'state_rglru': 2.726,
     'router_wg': 7.142,
     'router_we': 8.0,
     'moe_w_gate': 7.061,
     'moe_w_up': 6.415,
     'moe_w_down': 6.373}
    for name, (base, spread) in spreads.items():
        noise = np.random.default_rng([zlib.crc32(name.encode()), seed]).standard_normal(out[name].shape)
        drawn = base * np.exp(spread * noise) if base else spread * noise
        out[name] = __import__('jax').numpy.asarray(drawn.astype(out[name].dtype))
    for name, factor in factors.items():
        out[name] = (out[name] * factor).astype(out[name].dtype)
    return out
```

```python
import math
from contextlib import ExitStack

import numpy as np

import concourse.bass as bass
from concourse import mybir

P = 128
D = 1024
KT = D // P
NCTX, NLAT = 128, 512
NTOK = NCTX + NLAT
TT = NTOK // P
H, HD = 8, 64
GRID, ROWS = 64, 8
WIN_R, WIN_C = 8, 16
NHY = 256
NE, NG, EPG, FE = 16, 4, 4, 256
MIN_TILES = 2 * NTOK // P
MAX_TILES = 26
ALPHA = 2.0 ** 0.25
LN_EPS = 1e-5
HIDDEN = 64
FEATS = 33
WPC = 256
RING = 3
NMOD1 = 16
NMOD2 = 32
BIG = 1e30
DCPAD = 63
HALF = NTOK // 2
HROWS = (HALF - NCTX) // GRID
LATW = [256, 384, 384, 256]
KEY0 = [0, 0, 1, 2]
COLOFF = [0, -16, -16, -16]

_COLS = {}


def _layout():
    at = 0
    for name, n in (("b_mod", NMOD1), ("rg_cw", 8), ("rg_cb", 2), ("ba", 4), ("bx", 4), ("lam", 4), ("h0", 4),
                    ("hy_cw", 18), ("hy_cb", 6), ("hy_b1", 1), ("hy_b2", 1), ("freq", 2),
                    ("negt", 5), ("not0", 1), ("dc_lat", 1), ("ds_lat", 1), ("dc_ctx", 1), ("ds_ctx", 1),
                    ("iota4", 4), ("iota26", 26), ("even13", 13)):
        _COLS[name] = (at, n)
        at += n
    return at


NPAR = _layout()


def build(nc, t):
    F = mybir.dt.float32
    I32 = mybir.dt.int32
    ALU = mybir.AluOpType
    ACT = mybir.ActivationFunctionType
    AX = mybir.AxisListType
    V, S, G, T = nc.vector, nc.scalar, nc.gpsimd, nc.tensor

    ctx = ExitStack()
    with ctx:
        def sem(name):
            return ctx.enter_context(nc.semaphore(name))

        ARENA = 52900

        def split_view(name, at, *dims):
            with nc.sbuf_tensor(name + "_before", [P, at], F), \
                    nc.sbuf_tensor(name, [P, dims[0] * dims[1]], mybir.dt.float32r) as a:
                return a[:, :].rearrange("p (a b) -> p a b", a=dims[0])

        SM = 1504
        MTAT = SM + RING * KT * WPC
        UTLAT = MTAT + KT * NTOK + TT * D + 11264 + 4 * NTOK
        UTH = [split_view(f"u_high{k}", MTAT + k * NTOK, 1, NTOK)[:, 0, :] for k in range(KT)]
        UTL = [split_view(f"u_low{k}", UTLAT + k * NTOK, 1, NTOK)[:, 0, :] for k in range(KT)]
        WL = [split_view(f"w_low{q}", SM + q * KT * WPC, KT, WPC) for q in range(2)]
        WH = [split_view(f"w_high{q}", SM + 2 * KT * WPC + q * KT * P, KT, P) for q in range(2)]
        arena = ctx.enter_context(nc.sbuf_tensor("arena", [P, ARENA], F))
        eids = ctx.enter_context(nc.sbuf_tensor("expert_of_tile", [P, MAX_TILES], I32))
        npair = ctx.enter_context(nc.sbuf_tensor("tile_pairs", [P, 1], I32))
        slots = ctx.enter_context(nc.sbuf_tensor("slots", [P, 2 * TT], I32))
        tokid = ctx.enter_context(nc.sbuf_tensor("token_ids", [P, TT], I32))
        zeroid = ctx.enter_context(nc.sbuf_tensor("zero_ids", [P, MAX_TILES], I32))
        toks = ctx.enter_context(nc.sbuf_tensor("token_of_slot", [P, MAX_TILES], I32))
        tokc = ctx.enter_context(nc.sbuf_tensor("token_of_slot_now", [P, 2], I32))
        B = [ctx.enter_context(nc.psum_tensor(f"bank{i}", [P, 512], F)) for i in range(8)]

        class Region:

            def __init__(self, start, size):
                self.at, self.end = start, start + size

            def take(self, *dims):
                n = 1
                for d in dims:
                    n *= d
                a = arena[:, self.at:self.at + n]
                self.at += n
                assert self.at <= self.end, (self.at, self.end)
                if len(dims) == 2:
                    a = a.rearrange("p (a b) -> p a b", a=dims[0])
                elif len(dims) == 3:
                    a = a.rearrange("p (a b c) -> p a b c", a=dims[0], b=dims[1])
                return a

        base = Region(0, 1700)
        ident = base.take(P)
        upper = base.take(P)
        ones = base.take(P)
        params = base.take(NPAR)
        cond = base.take(KT, 2)
        sig = base.take(KT, 2)
        wrt = base.take(KT, NG + NE)
        brt = base.take(NG + NE)
        modc = base.take(2 * NMOD1)
        stats = base.take(TT, 12)
        mv = base.take(TT, 2)
        rstd = base.take(TT)
        nmr = base.take(TT)
        soft = base.take(3, 40)
        sp = base.take(8, 4)
        hstate = base.take(4)
        hbias = base.take(8)
        wts = base.take(TT, 2)
        tidf = base.take(1)
        assert base.at <= SM, base.at
        ringr = Region(SM, RING * KT * WPC)
        ring = [ringr.take(KT, WPC) for _ in range(RING)]
        assert MTAT == ringr.at
        MT = Region(MTAT, KT * NTOK).take(KT, NTOK)
        LATE = MTAT + KT * NTOK

        xr_ = Region(LATE, TT * D)
        X = xr_.take(TT, D)
        xr2 = Region(LATE, TT * D)
        HYT = xr2.take(TT, 3 * NHY)
        GATE = xr2.take(2, NTOK)
        h1 = Region(xr_.end, 11264)
        HC = h1.take(4, 512)
        HS = h1.take(4, 512)
        HDm = h1.take(512)
        HCc = h1.take(512)
        HSc = h1.take(512)
        HDc = h1.take(512)
        RT = h1.take(4, 2, NTOK)
        RTC = RT.rearrange("p a b c -> p (a b c)")
        UTF = RTC.rearrange("p (k n) -> p k n", k=KT)
        mrow1 = RTC[0:2, 0:P * NMOD1]
        mrow2 = RTC[0:2, 0:P * NMOD2]
        h2 = Region(xr_.end, 11264)
        BM = [h2.take(4, 384) for _ in range(2)]
        masks = h2.take(256 + 384 + 256)
        TS = [h2.take(512) for _ in range(2)]
        PR = [h2.take(512) for _ in range(2)]
        PTs = [h2.take(512) for _ in range(2)]
        OS = [h2.take(512) for _ in range(2)]
        assert h2.at + D <= h1.end
        ZERO = arena[:, h1.end - D:h1.end]
        f1 = Region(h1.end, 11532)
        EV = f1.take(TT, 512)
        OD = f1.take(TT, 512)
        WN = f1.take(D)
        HF = f1.take(NTOK)
        FA = f1.take(NTOK)
        FB = f1.take(NTOK)
        feats = f1.take(NTOK)
        decay = f1.take(D)
        w3 = f1.take(D)
        w1 = f1.take(HIDDEN)
        w2 = f1.take(HIDDEN)
        NXR = NTOK + 6
        f2 = Region(h1.end, 11532)
        VC = arena[:, f2.at:f2.at + 4 * NTOK].rearrange("p (a b) -> p a b", a=4)
        assert UTLAT == f2.at + 4 * NTOK
        ZA = f2.take(TT, NHY)
        ZB = f2.take(TT, NHY)
        YA = f2.take(TT, NHY)
        YB = f2.take(TT, NHY)
        VT = f2.take(TT, 512)
        KTt = f2.take(4, NTOK)
        XRP = f2.take(2, NXR)
        NK = XRP.rearrange("p a b -> p (a b)")[:, 0:512]
        q_ = Region(f1.end, 20000)
        NHP = NTOK + 4
        qh = Region(q_.at, 4 * NHP)
        HYP = [qh.take(NHP) for _ in range(2)]
        HYC = [qh.take(NHP) for _ in range(2)]
        QT = q_.take(4, NTOK)
        q_.at = qh.end
        cKT = q_.take(4, P)
        cV = q_.take(512)
        XC = q_.take(2, NXR - 3)
        dft = q_.take(5504)
        Cm = dft[:, 0:2048].rearrange("p (a b) -> p a b", a=4)
        Sm = dft[:, 2048:4096].rearrange("p (a b) -> p a b", a=4)
        Sf = dft[:, 4096:4608].rearrange("p (a b) -> p a b", a=4)
        Si = dft[:, 4608:5120]
        Cc = dft[:, 5120:5248]
        Sfc = dft[:, 5248:5376]
        Sic = dft[:, 5376:5504]
        skip = q_.take(512)
        rgw = q_.take(8, P)
        assert q_.at <= ARENA, q_.at

        wor = Region(ARENA - 4 * KT * WPC, 4 * KT * WPC)
        wo = [wor.take(KT, WPC) for _ in range(4)]
        assert wor.end - 4 * KT * WPC >= qh.end + 2 * 512
        moe = Region(ARENA - 4 * KT * WPC, 4 * KT * WPC)
        xg = [moe.take(D) for _ in range(2)]
        xgT = [moe.take(KT, P) for _ in range(2)]
        hh = [moe.take(2, FE) for _ in range(2)]
        hT = [moe.take(2, P) for _ in range(2)]
        yy = [moe.take(D) for _ in range(2)]
        late = Region(LATE, ARENA - 4 * KT * WPC - LATE)
        X1 = late.take(TT, D)
        g2b = late.take(2, D)
        l2g = late.take(D)
        l2b = late.take(D)
        LO = late.take(TT, 20)
        OG, LT, LG, ES, O1, O2 = (late.take(TT, 4) for _ in range(6))
        GM, L1, M1, M2, DL = (late.take(TT) for _ in range(5))
        E44, E1, E2 = (late.take(TT, 4, 4) for _ in range(3))
        MH, SL, SX = (late.take(TT, NE) for _ in range(3))
        TC, TI = (late.take(NE) for _ in range(2))
        EI = late.take(MAX_TILES, NE)
        EJ = late.take(MAX_TILES)
        lateA = late.at
        g1b = late.take(2, D)
        l1g = late.take(D)
        l1b = late.take(D)
        sh2b = late.take(2, D)
        sc2b = late.take(2, D)
        U2 = late.take(TT, D)
        U2T = late.take(KT, NTOK)
        wdn1 = late.take(2, D)
        last_ = Region(lateA, late.at - lateA)
        ga = last_.take(TT, D)
        gb = last_.take(TT, D)
        wreg = Region(SM, RING * KT * WPC + KT * NTOK)
        wgu = [wreg.take(KT, 2 * FE) for _ in range(2)]
        wdn = [wreg.take(2, D), wdn1]
        YAc, YBc = YA[:, 4, :], YB[:, 4, :]

        def ycols(ft):
            return YA[:, ft, :], YB[:, ft, :], ZA[:, ft, :], ZB[:, ft, :]

        def skz(i):
            return ZA[:, i, :]

        def col(name, i=0, rows=P):
            a = _COLS[name][0] + i
            return params[0:rows, a:a + 1]

        ld_small = sem("ld_small")
        ld_filt = sem("ld_filt")
        ld_dft = sem("ld_dft")
        ld_x = [sem(f"ld_x{i}") for i in range(TT)]
        ld_attn = sem("ld_attn")
        ring_in = [sem(f"ring_in{i}") for i in range(RING)]
        piece_used = sem("piece_used")
        dv = sem("vector_step")
        ac = sem("scalar_step")
        po = sem("pool_step")
        filt_mm = sem("filt_mm")
        filt_arg = sem("filt_arg")
        filt_sin = sem("filt_sin")
        win_rdy = sem("win_rdy")
        h3_mm = sem("h3_mm")
        eo_rdy = sem("eo_rdy")
        spec_mm = sem("spec_mm")
        spec_ev = sem("spec_ev")
        modc_rdy = sem("modc_rdy")
        cond_rdy = sem("cond_rdy")
        var_rdy = sem("var_rdy")
        std_rdy = sem("std_rdy")
        xhat_rdy = sem("xhat_rdy")
        ut_mm = sem("ut_mm")
        ut_lat = sem("ut_lat")
        ut_ctx = sem("ut_ctx")
        uth_rdy = sem("uth_rdy")
        utl_rdy = sem("utl_rdy")
        wh_rdy = sem("wh_rdy")
        wl_rdy = sem("wl_rdy")
        proj_mm = sem("proj_mm")
        proj_lat = sem("proj_lat")
        proj_ctx = sem("proj_ctx")
        v_mm = sem("v_mm")
        v_ev = sem("v_ev")
        pads = sem("pads")
        hyc_rdy = sem("hyc_rdy")
        hyt_mm = sem("hyt_mm")
        hyt_ev = sem("hyt_ev")
        xc_rdy = sem("xc_rdy")
        rg_mm = sem("rg_mm")
        rg_th = sem("rg_th")
        rg_la = sem("rg_la")
        rg_au = sem("rg_au")
        rg_q = sem("rg_q")
        rg_sq = sem("rg_sq")
        rg_out = sem("rg_out")
        gel_in = sem("gel_in")
        gel_th = sem("gel_th")
        nk_mm = sem("nk_mm")
        nk_ev = sem("nk_ev")
        z_mm = sem("z_mm")
        z_ev = sem("z_ev")
        y_rdy = sem("y_rdy")
        inv_mm = sem("inv_mm")
        z_next = sem("z_next")
        hyo_mm = sem("hyo_mm")
        hyo_ev = sem("hyo_ev")
        m1_ev = sem("m1_ev")
        m1_mm = sem("m1_mm")
        mb_in = sem("mb_in")
        mr_ev = sem("mr_ev")
        mr_st = sem("mr_st")
        bm_in = [sem("bm_in0"), sem("bm_in1")]
        bm_rdy = sem("bm_rdy")
        s_mm = sem("s_mm")
        s_read = sem("s_read")
        mx_rdy = sem("mx_rdy")
        p_rdy = sem("p_rdy")
        pt_mm = sem("pt_mm")
        pt_ev = sem("pt_ev")
        pv_mm = sem("pv_mm")
        o_rdy = sem("o_rdy")
        ot_mm = sem("ot_mm")
        ot_ev = sem("ot_ev")
        ld_late = sem("ld_late")
        mix_mm = sem("mix_mm")
        mix_ev = sem("mix_ev")
        l1_var = sem("l1_var")
        l1_std = sem("l1_std")
        l1b_var = sem("l1b_var")
        l1b_std = sem("l1b_std")
        u2_rdy = sem("u2_rdy")
        u2_st = sem("u2_st")
        u2t_mm = sem("u2t_mm")
        u2t_ev = sem("u2t_ev")
        lg_mm = sem("lg_mm")
        gexp_in = sem("gexp_in")
        gexp = sem("gexp")
        pexp_in = sem("pexp_in")
        pexp = sem("pexp")
        onehot = sem("onehot")
        rank_mm = sem("rank_mm")
        slots_rdy = sem("slots_rdy")
        tokc_rdy = sem("tokc_rdy")
        zero_st = sem("zero_st")
        scat = sem("scat")
        tok_in = sem("tok_in")
        wgu_in = [sem("wgu_in0"), sem("wgu_in1")]
        wdn_in = [sem("wdn_in0"), sem("wdn_in1")]
        xg_in = [sem("xg_in0"), sem("xg_in1")]
        xt_mm = sem("xt_mm")
        gu_mm = sem("gu_mm")
        th_rdy = sem("th_rdy")
        h_rdy = sem("h_rdy")
        ht_mm = sem("ht_mm")
        ht_ev = sem("ht_ev")
        dn_mm = sem("dn_mm")
        y_st = [sem("y_st0"), sem("y_st1")]
        y_all = sem("y_all")
        ga_in = [sem(f"ga_in{i}") for i in range(TT)]
        l2_var = sem("l2_var")
        l2_std = sem("l2_std")
        fin_rdy = sem("fin_rdy")
        fin_last = sem("fin_last")
        out_st = sem("out_st")
        k_st = sem("k_st")
        modc_in = sem("modc_in")
        sp_in = sem("sp_in")
        sp_exp = sem("sp_exp")
        eo_win = sem("eo_win")
        xhat_in = sem("xhat_in")
        sk_rdy = sem("sk_rdy")
        mask_in = sem("mask_in")
        ld_g1 = sem("ld_g1")
        ld_g2 = sem("ld_g2")
        ga_w = sem("ga_w")
        l2_nmr = sem("l2_nmr")
        l2_xhat = sem("l2_xhat")
        xt_evA = sem("xt_evA")
        xt_evB = sem("xt_evB")
        y_evA = sem("y_evA")
        y_evB = sem("y_evB")
        hg_rdy = sem("hg_rdy")
        rg_fin = sem("rg_fin")
        yz_rdy = sem("yz_rdy")
        yz_st = sem("yz_st")
        wo_in = sem("wo_in")
        pool_turn = sem("pool_turn")

        mod_scr, u2_scr, tok_scr, y_scr = t["mod_scr"], t["u2_scr"], t["tok_scr"], t["y_scr"]

        hy0, xr0, gate0, q0, k0, v0 = 2048, 1536, 1792, 0, 512, 1024
        pieces = [("w_mod", WPC * i) for i in range(8)]
        pieces += [("w_in", hy0), ("w_in", hy0 + 256), ("w_in", hy0 + 512), ("w_in", xr0), ("w_in", gate0),
                   ("w_in", q0), ("w_in", q0 + 256), ("w_in", k0), ("w_in", k0 + 256),
                   ("w_in", v0), ("w_in", v0 + 256)]
        pieces += [("w_mod", 2048 + WPC * i) for i in range(16)]

        def wait_used(eng, p):
            if p < 8:
                eng.wait_ge(piece_used, p + 1)
            elif p < 19:
                eng.wait_ge(proj_mm, 2 * (p - 8) + 2)
            else:
                eng.wait_ge(piece_used, 8 + p - 18)

        slot_of = [n % 2 if 8 <= n < 19 else n % RING for n in range(len(pieces))]

        def wait_piece(eng, n):
            eng.wait_ge(ring_in[slot_of[n]], 16 * slot_of[:n + 1].count(slot_of[n]))

        def mod2_bank(p):
            return B[p % 3][0:2, 0:WPC]

        block = ctx.enter_context(nc.Block())

        @block.sync
        def _(eng):
            eng.wait_ge(ld_filt, 16 * 5)
            for n, (name, c0) in enumerate(pieces):
                former = [q for q in range(n) if slot_of[q] == slot_of[n]]
                if n == 20:
                    wait_used(eng, 18)
                elif former:
                    wait_used(eng, former[-1])
                eng.dma_start(ring[slot_of[n]][:, :, :],
                              t[name].rearrange("(k p) n -> p k n", p=P)[:, :, c0:c0 + WPC]
                              ).then_inc(ring_in[slot_of[n]], 16)
                if 3 <= n < 3 + TT:
                    i = n - 3
                    eng.dma_start(X[:, i, :], t["x"][i * P:(i + 1) * P, :]).then_inc(ld_x[i], 16)
            eng.wait_ge(hyo_mm, 2)
            eng.wait_ge(rg_fin, 1)
            for p in range(4):
                eng.dma_start(wo[p], t["w_out"].rearrange("(k p) n -> p k n", p=P)[:, :, p * WPC:(p + 1) * WPC]
                              ).then_inc(wo_in, 16)
            eng.wait_ge(yz_rdy, 1)
            for k in range(MIN_TILES, MAX_TILES):
                eng.dma_start(y_scr[k * P:(k + 1) * P, :], ZERO).then_inc(yz_st, 16)
            eng.wait_ge(ot_ev, 5)
            eng.wait_ge(hyo_ev, 4)
            eng.wait_ge(k_st, 48)
            eng.wait_ge(yz_st, 16 * (MAX_TILES - MIN_TILES))
            for i in range(TT):
                eng.dma_start(X1[:, i, :], t["x"][i * P:(i + 1) * P, :]).then_inc(ld_x[i], 16)
            eng.wait_ge(mix_mm, 2 * TT)
            eng.wait_ge(slots_rdy, 2)
            np_ = eng.value_load(npair[0:1, 0:1], min_val=1, max_val=MAX_TILES // 2)
            with eng.Fori(0, np_) as i:
                for j in range(2):
                    e = eng.value_load(eids[0:1, bass.ds(i * 2 + j, 1)], min_val=0, max_val=NE - 1)
                    row = eng.snap(e * D)
                    rowd = eng.snap(e * FE)
                    free = eng.snap(i * 2 + j + 1)
                    eng.wait_ge(gu_mm, free)
                    eng.dma_start(wgu[j][:, :, 0:FE],
                                  t["moe_w_gate"][bass.ds(row, D), :].rearrange("(k p) n -> p k n", p=P)
                                  ).then_inc(wgu_in[j], 16)
                    eng.dma_start(wgu[j][:, :, FE:2 * FE],
                                  t["moe_w_up"][bass.ds(row, D), :].rearrange("(k p) n -> p k n", p=P)
                                  ).then_inc(wgu_in[j], 16)
                    eng.wait_ge(tok_in, 16)
                    eng.wait_ge(dn_mm, free)
                    eng.dma_start(wdn[j][:, :, :],
                                  t["moe_w_down"][bass.ds(rowd, FE), :].rearrange("(k p) n -> p k n", p=P)
                                  ).then_inc(wdn_in[j], 16)
            for i in range(TT):
                if i < TT - 1:
                    eng.wait_ge(fin_rdy, i + 1)
                else:
                    eng.wait_ge(fin_last, 1)
                eng.dma_start(t["y"][i * P:(i + 1) * P, :], X1[:, i, :]).then_inc(out_st, 16)
            eng.wait_ge(out_st, 16 * TT)

        @block.gpsimd
        def _(eng):
            count = {}

            def after(s, v=1):
                count[s] = count.get(s, 0) + v
                eng.wait_ge(s, count[s])

            def step(ins):
                ins.then_inc(po, 1)
                after(po)

            step(G.memset(zeroid[:, :], 0))
            for c in range(2):
                for a, b in ((0, 1), (1 + NCTX, 3 + NCTX), (NHP - 1, NHP)):
                    step(G.memset(HYP[c][:, a:b], 0.0))
            eng.sem_inc(pads, 1)
            eng.dma_start(tok_scr.rearrange("(p a) b -> p (a b)", p=P), zeroid[:, :]).then_inc(zero_st, 16)
            eng.wait_ge(spec_ev, 12)
            for c in range(2):
                for a, b in ((0, 2), (2 + NCTX, 5 + NCTX), (NXR - 1, NXR)):
                    step(G.memset(XRP[:, c, a:b], 0.0))
            eng.sem_inc(pads, 1)

            def low_half(m):
                eng.wait_ge(wh_rdy, m + 1)
                w = slice((m % 2) * P, (m % 2 + 1) * P)
                s_ = slot_of[8 + m // 2]
                G.tensor_tensor(WL[s_][:, :, w], ring[s_][:, :, w], WH[m % 2].bitcast(F), ALU.subtract
                                ).then_inc(wl_rdy, 1)

            for m in range(13):
                low_half(m)
            g3 = XRP[:, :, 0:NTOK]
            eng.wait_ge(proj_lat, 10)
            eng.wait_ge(proj_ctx, 10)
            eng.wait_ge(xc_rdy, 1)
            step(G.tensor_tensor(g3, GATE[:, :, :], GATE[:, :, :], ALU.mult))
            step(G.tensor_scalar(g3, g3, 0.044715, 1.0, ALU.mult, ALU.add))
            G.tensor_tensor(g3, g3, GATE[:, :, :], ALU.mult).then_inc(gel_in, 1)
            after(gel_in)
            for m in range(13, 15):
                low_half(m)
            eng.wait_ge(gel_th, 1)
            step(G.tensor_scalar(g3, g3, 1.0, None, ALU.add))
            G.tensor_tensor(GATE[:, :, :], GATE[:, :, :], g3, ALU.mult).then_inc(gel_in, 1)
            after(gel_in)

            for m in range(15, 22):
                low_half(m)

            eng.wait_ge(ld_attn, 16 * 4)
            for o in range(2):
                for ft in range(5):
                    eng.wait_ge(z_ev, 5 * o + ft + 1)
                    ya, yb, za, zb = ycols(ft)
                    step(G.tensor_tensor(ya, ya, za, ALU.subtract))
                    G.tensor_tensor(yb, yb, zb, ALU.add).then_inc(y_rdy, 1)
                    after(y_rdy)
                eng.wait_ge(y_rdy, 5 * o + 5)
                for tt in range(TT):
                    if o == 1:
                        eng.wait_ge(z_next, 5)
                    G.tensor_tensor(skz(tt), HYT[:, tt, 0:NHY], skip[:, o * NHY:(o + 1) * NHY], ALU.mult
                                    ).then_inc(sk_rdy, 1)
                    after(sk_rdy)

            moff = [0, 256, 256, 640]
            for g in range(8):
                b = g // 2
                nk = LATW[b]
                if g == 0:
                    eng.wait_ge(rg_out, 2)
                    eng.wait_ge(y_rdy, 10)
                    eng.wait_ge(rg_fin, 1)
                    G.memset(ZERO, 0.0).then_inc(yz_rdy, 1)
                    eng.dma_start(masks, t["masks"]).then_inc(mask_in, 16)
                    eng.wait_ge(mask_in, 16)
                if g >= 2:
                    eng.wait_ge(s_read, 8 + 4 * (g - 1))
                for h in range(4):
                    head = 4 * (g % 2) + h
                    src = bass.AP(t["rpb"].tensor, head * ROWS * DCPAD * 8 + (COLOFF[b] + 16) * 8,
                                  [[8, 16], [DCPAD * 8, ROWS], [1, nk]])
                    eng.dma_start(BM[g % 2][:, h, 0:nk], src).then_inc(bm_in[g % 2], 16)
                eng.wait_ge(bm_in[g % 2], 64 * (g // 2 + 1))
                for h in range(4):
                    step(G.tensor_tensor(BM[g % 2][:, h, 0:nk], BM[g % 2][:, h, 0:nk],
                                         masks[:, moff[b]:moff[b] + nk], ALU.add))
                eng.sem_inc(bm_rdy, 1)

            for i in range(TT):
                eng.wait_ge(u2_rdy, i + 1)
                eng.dma_start(u2_scr[i * P:(i + 1) * P, :], U2[:, i, :]).then_inc(u2_st, 16)
            eng.wait_ge(slots_rdy, 2)
            eng.wait_ge(zero_st, 16)
            for i in range(TT):
                for s in range(2):
                    eng.indirect_dma_start(tok_scr, bass.IndirectOffsetOnAxis(ap=slots[:, 2 * i + s:2 * i + s + 1], axis=0),
                                           tokid[:, i:i + 1], None).then_inc(scat, 16)
            eng.wait_ge(scat, 32 * TT)
            eng.dma_start(toks[:, :], tok_scr.rearrange("(a p) b -> p (a b)", p=P),
                          allow_slow_non_contiguous=True).then_inc(tok_in, 16)
            eng.wait_ge(tok_in, 16)
            eng.wait_ge(u2_st, 16 * TT)
            np_ = eng.value_load(npair[0:1, 0:1], min_val=1, max_val=MAX_TILES // 2)
            with eng.Fori(0, np_) as i:
                for j in range(2):
                    free = eng.snap(i * 2 + j + 1)
                    eng.wait_ge(xt_mm, free)
                    eng.sem_inc(pool_turn, 1)
                    G.tensor_copy(tokc[:, j:j + 1], toks[:, bass.ds(i * 2 + j, 1)]).then_inc(tokc_rdy, 1)
                    eng.wait_ge(tokc_rdy, free)
                    eng.sem_inc(pool_turn, 1)
                    eng.indirect_dma_start(xg[j][:, :], None, u2_scr,
                                           bass.IndirectOffsetOnAxis(ap=tokc[:, j:j + 1], axis=0)).then_inc(xg_in[j], 16)
            total = eng.snap(np_ * 16 + 16)
            eng.wait_ge(y_st[0], total)
            eng.sem_inc(y_all, 1)
            eng.wait_ge(y_st[1], total)
            eng.sem_inc(y_all, 1)
            for i in range(TT):
                for s, dst in enumerate((ga, gb)):
                    eng.indirect_dma_start(dst[:, i, :], None, y_scr,
                                           bass.IndirectOffsetOnAxis(ap=slots[:, 2 * i + s:2 * i + s + 1], axis=0)
                                           ).then_inc(ga_in[i], 16)
            for i in range(TT - 1):
                eng.wait_ge(l2_xhat, i + 1)
                step(G.tensor_tensor(X1[:, i, :], X1[:, i, :], l2g, ALU.mult))
                G.tensor_tensor(X1[:, i, :], X1[:, i, :], l2b, ALU.add).then_inc(fin_rdy, 1)
                after(fin_rdy)

        @block.scalar
        def _(eng):
            count = {}

            def after(s, v=1):
                count[s] = count.get(s, 0) + v
                eng.wait_ge(s, count[s])

            def step(ins):
                ins.then_inc(ac, 1)
                after(ac)

            for dst, name in ((ident, "ident"), (upper, "upper"), (ones, "ones"), (params, "params"),
                              (cond, "cond"), (wrt, "wrt")):
                eng.dma_start(dst, t[name]).then_inc(ld_small, 16)
            eng.dma_start(brt, t["brt"].partition_broadcast(P)).then_inc(ld_small, 16)
            eng.dma_start(tokid[:, :], t["tokid"]).then_inc(ld_small, 16)
            eng.dma_start(feats[0:FEATS, :], t["feats"]).then_inc(ld_filt, 16)
            eng.dma_start(w1[0:FEATS, :], t["hy_w1"]).then_inc(ld_filt, 16)
            eng.dma_start(w2[0:HIDDEN, :], t["hy_w2"]).then_inc(ld_filt, 16)
            eng.dma_start(w3[0:HIDDEN, :], t["hy_w3"]).then_inc(ld_filt, 16)
            eng.dma_start(decay, t["decay"].partition_broadcast(P)).then_inc(ld_filt, 16)
            eng.wait_ge(ld_small, 16 * 8)
            S.activation(sig, cond, ACT.Tanh, scale=0.5).then_inc(cond_rdy, 1)
            after(cond_rdy)
            eng.wait_ge(sp_in, 1)
            S.activation(sp[:, 1, :], sp[:, 1, :], ACT.Exp, scale=-1.0).then_inc(sp_exp, 1)
            after(sp_exp)
            for layer in range(2):
                eng.wait_ge(filt_arg, layer + 1)
                S.activation(HF[0:HIDDEN, :], FA[0:HIDDEN, :], ACT.Sin).then_inc(filt_sin, 1)
                after(filt_sin)
                for b in (2 * layer, 2 * layer + 1):
                    eng.wait_ge(piece_used, 2 * b + 2)
                    S.activation(mrow1[:, 512 * b:512 * (b + 1)], B[4 + b][0:2, :], ACT.Copy).then_inc(m1_ev, 1)
                    after(m1_ev)
            eng.dma_start(dft, t["dft"]).then_inc(ld_dft, 16)
            eng.dma_start(cKT, t["cache_kT"]).then_inc(ld_attn, 16)
            eng.dma_start(cV, t["cache_v"]).then_inc(ld_attn, 16)
            eng.dma_start(rgw, t["rgw"]).then_inc(ld_attn, 16)
            eng.dma_start(skip, t["skip"].partition_broadcast(P)).then_inc(ld_attn, 16)
            eng.wait_ge(ld_filt, 16 * 5)
            step(S.activation(decay, decay, ACT.Abs))
            for i in range(TT):
                if i >= 1:
                    eng.wait_ge(eo_win, i)
                S.activation(WN, decay, ACT.Exp, scale=col("negt", i)).then_inc(win_rdy, 1)
                after(win_rdy)
            def x_hat(tiles):
                eng.wait_ge(xhat_in, 1)
                for i in tiles:
                    S.activation(X[:, i, :], X[:, i, :], ACT.Identity, scale=rstd[:, i:i + 1], bias=nmr[:, i:i + 1]
                                 ).then_inc(xhat_rdy, 1)
                    after(xhat_rdy)

            def high_half(m):
                if m < 2:
                    eng.wait_ge(piece_used, 6)
                else:
                    eng.wait_ge(proj_mm, m - 1)
                wait_piece(eng, 8 + m // 2)
                S.activation(WH[m % 2], ring[slot_of[8 + m // 2]][:, :, (m % 2) * P:(m % 2 + 1) * P], ACT.Copy
                             ).then_inc(wh_rdy, 1)

            g = 0
            for ft in range(4):
                g += 1
                eng.wait_ge(spec_mm, g)
                if ft == 0:
                    step(S.activation(HDm, B[(g - 1) % 4][:, :], ACT.Copy, scale=col("dc_lat")))
                S.activation(HC[:, ft, :], B[(g - 1) % 4][:, :], ACT.Copy,
                             scale=col("dc_lat") if ft == 0 else 2.0 / (2 * NLAT)).then_inc(spec_ev, 1)
                after(spec_ev)
                g += 1
                eng.wait_ge(spec_mm, g)
                S.activation(HS[:, ft, :], B[(g - 1) % 4][:, :], ACT.Copy,
                             scale=col("ds_lat") if ft == 0 else 2.0 / (2 * NLAT)).then_inc(spec_ev, 1)
                after(spec_ev)
                if ft == 0:
                    eng.wait_ge(var_rdy, 1)
                    S.activation(rstd, rstd, ACT.Sqrt).then_inc(std_rdy, 1)
                    after(std_rdy)
                else:
                    x_hat(((0, 1), (2, 3), (4,))[ft - 1])
            eng.wait_ge(spec_mm, 9)
            S.activation(HDm[0:1, :], B[0][0:1, :], ACT.Copy, scale=1.0 / (2 * NLAT)).then_inc(spec_ev, 1)
            after(spec_ev)
            eng.wait_ge(spec_mm, 10)
            step(S.activation(HDc, B[1][:, :], ACT.Copy, scale=col("dc_ctx")))
            S.activation(HCc, B[1][:, :], ACT.Copy, scale=col("dc_ctx")).then_inc(spec_ev, 1)
            after(spec_ev)
            eng.wait_ge(spec_mm, 11)
            S.activation(HSc, B[2][:, :], ACT.Copy, scale=col("ds_ctx")).then_inc(spec_ev, 1)
            after(spec_ev)
            eng.wait_ge(spec_mm, 12)
            S.activation(HDc[0:1, :], B[3][0:1, :], ACT.Copy, scale=1.0 / (2 * NCTX)).then_inc(spec_ev, 1)
            after(spec_ev)
            high_half(0)
            high_half(1)
            eng.wait_ge(modc_rdy, 1)
            for k in range(KT):
                eng.wait_ge(ut_mm, k + 1)
                S.activation(UTF[:, k, NCTX:NTOK], B[5 + k % 2][:, :], ACT.Identity,
                             scale=modc[:, 2 * (8 + k) + 1:2 * (8 + k) + 2], bias=modc[:, 2 * k + 1:2 * k + 2]
                             ).then_inc(ut_lat, 1)
                after(ut_lat)
                eng.wait_ge(ut_ctx, k + 1)
                S.activation(UTH[k], UTF[:, k, :], ACT.Copy).then_inc(uth_rdy, 1)
                after(uth_rdy)
            lb = [B[1], B[2]]

            def hyt_copy(c):
                eng.wait_ge(hyt_mm, c + 1)
                step(S.activation(HYT[:, 1:TT, c * P:(c + 1) * P],
                                  B[5][:, :].rearrange("p (t c) -> p t c", t=4), ACT.Copy))
                S.activation(HYT[:, 0, c * P:(c + 1) * P], B[6][:, 0:P], ACT.Copy).then_inc(hyt_ev, 1)
                after(hyt_ev)

            def rg_tanh(c):
                for m in range(4 * c, 4 * c + 4):
                    gate, e = (m % 4) // 2, m % 2
                    eng.wait_ge(rg_mm, m + 1)
                    if m == 4 * c and c == 1:
                        eng.wait_ge(rg_out, 1)
                    hb = hbias[:, 4 * gate + 2 * e + c:4 * gate + 2 * e + c + 1]
                    step(S.activation(RT[:, gate, e, NCTX:NTOK], B[7 if m % 2 == 0 else 0][:, :], ACT.Tanh,
                                      scale=0.5, bias=hb))
                    S.activation(RT[:, gate, e, 0:NCTX], B[5 + m % 2][:, 0:NCTX], ACT.Tanh,
                                 scale=0.5, bias=hb).then_inc(rg_th, 1)
                    after(rg_th)

            def rg_exp(c):
                eng.wait_ge(rg_la, c + 1)
                step(S.activation(RT[:, 2, :, :], RT[:, 0, :, :], ACT.Tanh, scale=-1.0))
                S.activation(RT[:, 0, :, :], RT[:, 0, :, :], ACT.Exp).then_inc(rg_au, 1)
                after(rg_au)

            def rg_root(c):
                eng.wait_ge(rg_q, c + 1)
                S.activation(RT[:, 2, :, :], RT[:, 2, :, :], ACT.Sqrt, scale=2.0).then_inc(rg_sq, 1)
                after(rg_sq)

            for m in range(22):
                eng.wait_ge(proj_mm, m + 1)
                if m + 2 < 22:
                    high_half(m + 2)
                src = lb[m % 2][:, 0:HALF]
                grid = src.rearrange("p (r c) -> p r c", r=ROWS - HROWS)
                if m < 6:
                    if m < 2:
                        eng.wait_ge(pads, 1)
                    else:
                        eng.wait_ge(hyc_rdy, m - 1)
                    S.activation(HYP[m % 2][:, 3 + HALF:3 + NTOK], src, ACT.Copy).then_inc(proj_lat, 1)
                    after(proj_lat)
                elif m < 8:
                    S.activation(XRP[:, m - 6, 5 + HALF:5 + NTOK], src, ACT.Copy).then_inc(proj_lat, 1)
                    after(proj_lat)
                elif m < 10:
                    S.activation(GATE[:, m - 8, HALF:NTOK], src, ACT.Copy).then_inc(proj_lat, 1)
                    after(proj_lat)
                elif m >= 18:
                    step(S.activation(VC[:, m - 18, 0:NCTX], B[3 + m % 2][:, 0:NCTX], ACT.Copy))
                    view = VC[:, m - 18, NCTX:NTOK].rearrange("p (c r) -> p r c", r=ROWS)
                    step(S.activation(view[:, 0:HROWS, :],
                                      B[3 + m % 2][:, NCTX:HALF].rearrange("p (r c) -> p r c", r=HROWS), ACT.Copy))
                    S.activation(view[:, HROWS:ROWS, :], grid, ACT.Copy).then_inc(proj_lat, 1)
                    after(proj_lat)
                else:
                    dst, c, sc = (QT, m - 10, 0.125) if m < 14 else (KTt, m - 14, 1.0)
                    view = dst[:, c, NCTX:NTOK].rearrange("p (c r) -> p r c", r=ROWS)
                    S.activation(view[:, HROWS:ROWS, ::-1] if m < 14 else view[:, HROWS:ROWS, :],
                                 grid, ACT.Copy, scale=sc).then_inc(proj_lat, 1)
                    after(proj_lat)
                if 2 <= m < 8:
                    hyt_copy(m - 2)
                if m == 11:
                    eng.wait_ge(gel_in, 1)
                    g3 = XRP[:, :, 0:NTOK]
                    S.activation(g3, g3, ACT.Tanh, scale=0.7978845608028654).then_inc(gel_th, 1)
                    after(gel_th)
                if m == 13:
                    rg_tanh(0)
                if m == 17:
                    rg_exp(0)
                if m == 18:
                    rg_root(0)
            rg_tanh(1)
            for i in range(TT):
                eng.wait_ge(v_mm, i + 1)
                S.activation(VT[:, i, :], B[1 + i % 4][:, :], ACT.Copy).then_inc(v_ev, 1)
                after(v_ev)
            eng.wait_ge(nk_mm, 1)
            eng.wait_ge(gel_in, 2)
            S.activation(NK, B[1][:, :], ACT.Copy).then_inc(nk_ev, 1)
            after(nk_ev)
            rg_exp(1)
            rg_root(1)
            eng.wait_ge(nk_ev, 1)
            eng.dma_start(t["new_k"], NK).then_inc(k_st, 16)
            eng.wait_ge(v_ev, TT)
            eng.dma_start(t["new_v"], VT[:, 0, :]).then_inc(k_st, 16)
            eng.wait_ge(rg_fin, 1)
            eng.dma_start(t["new_state"], hstate).then_inc(k_st, 16)
            eng.dma_start(mrow2, t["b_mod2"].partition_broadcast(2)).then_inc(mb_in, 16)
            eng.wait_ge(mr_ev, 16)
            eng.dma_start(mod_scr, mrow2).then_inc(mr_st, 16)
            for c in range(2):
                eng.wait_ge(hyo_mm, c + 1)
                step(S.activation(MT[:, 6 + c, NCTX:NTOK], B[3 + c][:, :], ACT.Copy))
                S.activation(MT[:, 6 + c, 0:NCTX], B[5 + c][:, 0:NCTX], ACT.Copy).then_inc(hyo_ev, 2)
                after(hyo_ev, 2)
            def ot_copy(blk):
                eng.wait_ge(ot_mm, blk + 1)
                src = B[6 + blk % 2]
                if blk == 0:
                    S.activation(MT[:, 0:4, 0:NCTX], src[:, :].rearrange("p (k c) -> p k c", k=4), ACT.Copy
                                 ).then_inc(ot_ev, 1)
                    after(ot_ev)
                else:
                    for k in range(4):
                        last = S.activation(
                            MT[:, k, NCTX:NTOK].rearrange("p (r c) -> p c r", r=ROWS)[:, 16 * (blk - 1):16 * blk, :],
                            src[:, k * P:(k + 1) * P].rearrange("p (c r) -> p c r", r=ROWS)[:, ::-1, :], ACT.Copy)
                    last.then_inc(ot_ev, 1)
                    after(ot_ev)

            for u in range(40 + 1):
                if u < 40:
                    w = P if u < 8 else LATW[(u - 8) // 8] + P
                    eng.wait_ge(mx_rdy, u + 1)
                    if u == 0:
                        eng.wait_ge(mr_st, 16)
                    if u >= 2:
                        eng.wait_ge(pt_mm, u - 1)
                    S.activation(PR[u % 2][:, 0:w], TS[u % 2][:, 0:w], ACT.Exp, bias=soft[:, 0, u:u + 1],
                                 accum_out=soft[:, 1, u:u + 1]).then_inc(p_rdy, 1)
                    after(p_rdy)
                if u >= 1:
                    q = u - 1
                    w = P if q < 8 else LATW[(q - 8) // 8] + P
                    eng.wait_ge(pt_mm, q + 1)
                    if q >= 2:
                        eng.wait_ge(pv_mm, q - 1)
                    S.activation(PTs[q % 2][:, 0:w], B[2 + q % 2][:, 0:w], ACT.Copy).then_inc(pt_ev, 1)
                    after(pt_ev)
                    if q % 8 == 7 and q >= 15:
                        ot_copy(q // 8 - 1)
            ot_copy(4)
            eng.wait_ge(mr_st, 16)
            eng.wait_ge(ot_ev, 5)
            eng.wait_ge(hyo_ev, 4)
            eng.wait_ge(k_st, 48)
            eng.wait_ge(yz_st, 16 * (MAX_TILES - MIN_TILES))
            for c in range(2):
                eng.dma_start(g1b[:, c, :], mod_scr[c, 0:D].partition_broadcast(P)).then_inc(ld_g1, 16)
            for dst, name in ((l1g, "ln1_g"), (l1b, "ln1_b"), (l2g, "ln2_g"), (l2b, "ln2_b")):
                eng.dma_start(dst, t[name].partition_broadcast(P)).then_inc(ld_late, 16)
            for m, dst in ((1, sh2b), (2, sc2b), (3, g2b)):
                for c in range(2):
                    if m == 3 and c == 1:
                        break
                    eng.dma_start(dst[:, c, :], mod_scr[c, m * D:(m + 1) * D].partition_broadcast(P)
                                  ).then_inc(ld_late, 16)
            eng.dma_start(g2b[:, 1, :], mod_scr[1, 3 * D:4 * D].partition_broadcast(P)).then_inc(ld_g2, 16)

            def u2t_copy(i):
                for b in range(2):
                    eng.wait_ge(u2t_mm, 2 * i + b + 1)
                    S.activation(U2T[:, 4 * b:4 * b + 4, i * P:(i + 1) * P],
                                 B[4 + b][:, :].rearrange("p (a b) -> p a b", a=4), ACT.Copy).then_inc(u2t_ev, 1)
                    after(u2t_ev)

            for i in range(TT):
                eng.wait_ge(l1_var, i + 1)
                S.activation(rstd[:, i:i + 1], rstd[:, i:i + 1], ACT.Sqrt).then_inc(l1_std, 1)
                after(l1_std)
                eng.wait_ge(l1b_var, i + 1)
                S.activation(rstd[:, i:i + 1], rstd[:, i:i + 1], ACT.Sqrt).then_inc(l1b_std, 1)
                after(l1b_std)
                if i >= 1:
                    u2t_copy(i - 1)
            u2t_copy(4)
            eng.wait_ge(gexp_in, 1)
            S.activation(LG, LG, ACT.Exp).then_inc(gexp, 1)
            after(gexp)
            eng.wait_ge(pexp_in, 1)
            S.activation(DL, DL, ACT.Exp).then_inc(pexp, 1)
            after(pexp)

            eng.wait_ge(yz_st, 16 * (MAX_TILES - MIN_TILES))
            eng.sem_inc(y_st[0], 16)
            eng.sem_inc(y_st[1], 16)
            eng.sem_inc(ht_ev, 1)
            eng.sem_inc(y_evA, 2)
            eng.wait_ge(slots_rdy, 2)
            np_ = eng.value_load(npair[0:1, 0:1], min_val=1, max_val=MAX_TILES // 2)
            with eng.Fori(0, np_) as i:
                for j in range(2):
                    xt_done = eng.snap(i * 2 + j + 3)
                    one = eng.snap(i * 2 + j + 1)
                    eng.wait_ge(xt_mm, xt_done)
                    eng.wait_ge(gu_mm, one)
                    S.activation(xgT[j][:, 0:4, :], B[2 * j][:, :].rearrange("p (a b) -> p a b", a=4), ACT.Copy
                                 ).then_inc(xt_evA, 1)
                for j in range(2):
                    done = eng.snap(i * 2 + j + 3)
                    one = eng.snap(i * 2 + j + 1)
                    eng.wait_ge(gu_mm, done)
                    eng.wait_ge(ht_mm, one)
                    S.activation(hh[j][:, 0, :], B[4 + j][:, 0:FE], ACT.Tanh, scale=0.5).then_inc(th_rdy, 1)
                for j in range(2):
                    done = eng.snap(i * 2 + j + 3)
                    one = eng.snap(i * 2 + j + 1)
                    eng.wait_ge(ht_mm, done)
                    eng.wait_ge(dn_mm, one)
                    S.activation(hT[j][:, :, :], B[6][:, 0:2 * P].rearrange("p (a b) -> p a b", a=2), ACT.Copy
                                 ).then_inc(ht_ev, 1)
                for j in range(2):
                    done = eng.snap(i * 2 + j + 3)
                    st = eng.snap(i * 16 + 16)
                    row = eng.snap((i * 2 + j) * P)
                    eng.wait_ge(dn_mm, done)
                    eng.wait_ge(y_st[j], st)
                    S.activation(yy[j][:, 0:512], B[2 * j][:, :], ACT.Copy).then_inc(y_evA, 1)
                    eng.wait_ge(y_evA, done)
                    eng.wait_ge(y_evB, done)
                    eng.dma_start(y_scr[bass.ds(row, P), :], yy[j][:, :]).then_inc(y_st[j], 16)
            def first_expert(i):
                eng.wait_ge(ga_in[i], 32)
                S.activation(ga[:, i, :], ga[:, i, :], ACT.Copy, scale=wts[:, i, 0:1]).then_inc(ga_w, 1)
                after(ga_w)

            first_expert(0)
            first_expert(1)
            for i in range(TT):
                eng.wait_ge(l2_var, i + 1)
                S.activation(rstd[:, i:i + 1], rstd[:, i:i + 1], ACT.Sqrt).then_inc(l2_std, 1)
                after(l2_std)
                if i + 2 < TT:
                    first_expert(i + 2)
                if i == TT - 1:
                    break
                eng.wait_ge(l2_nmr, i + 1)
                S.activation(X1[:, i, :], X1[:, i, :], ACT.Identity, scale=rstd[:, i:i + 1], bias=nmr[:, i:i + 1]
                             ).then_inc(l2_xhat, 1)
                after(l2_xhat)

        @block.tensor
        def _(eng):
            mm = T.matmul

            def piece(p):
                wait_piece(eng, p)
                return ring[slot_of[p]]

            def rows(w, dst):
                for k in range(KT):
                    last = mm(dst, cond[:, k, :], w[:, k, :], start=(k == 0), stop=(k == KT - 1))
                last.then_inc(piece_used, 1)

            eng.wait_ge(ld_filt, 16 * 5)
            eng.wait_ge(ld_small, 16 * 8)
            for layer in range(2):
                if layer:
                    eng.wait_ge(filt_sin, 1)
                w = w2[0:HIDDEN, :] if layer else w1[0:FEATS, :]
                x = HF[0:HIDDEN, :] if layer else feats[0:FEATS, :]
                mm(B[2 * layer][0:HIDDEN, :], w, x[:, NCTX:NTOK], start=True, stop=True)
                mm(B[2 * layer + 1][0:HIDDEN, 0:NCTX], w, x[:, 0:NCTX], start=True, stop=True).then_inc(filt_mm, 1)
                if layer == 0:
                    eng.wait_ge(modc_in, 1)
                for p in range(4 * layer, 4 * layer + 4):
                    rows(piece(p), B[4 + p // 2][0:2, WPC * (p % 2):WPC * (p % 2 + 1)])
            for b in range(4):
                eng.wait_ge(m1_ev, b + 1)
                for a in range(4 * b, 4 * b + 4):
                    last = T.transpose(B[0][:, 2 * a:2 * a + 2], mrow1[:, a * P:(a + 1) * P], ident[0:2, 0:2])
            last.then_inc(m1_mm, 1)
            eng.wait_ge(filt_sin, 2)
            for i in range(TT):
                if i >= 2:
                    eng.wait_ge(eo_win, i - 1)
                for c in range(2):
                    last = mm(B[4 + 2 * (i % 2) + c][:, :], HF[0:HIDDEN, i * P:(i + 1) * P],
                              w3[0:HIDDEN, 512 * c:512 * (c + 1)], start=True, stop=True)
                last.then_inc(h3_mm, 1)
            eng.wait_ge(ld_dft, 16)
            eng.wait_ge(modc_rdy, 1)
            eng.wait_ge(eo_rdy, TT)
            g = 0

            def spec(lhs, parts, rows=P):
                nonlocal g
                if g >= 4:
                    eng.wait_ge(spec_ev, g - 3)
                for a, (l, r) in enumerate(zip(lhs, parts)):
                    last = mm(B[g % 4][0:rows, :], l, r, start=(a == 0), stop=(a == len(lhs) - 1))
                last.then_inc(spec_mm, 1)
                g += 1

            ev = [EV[:, 1 + a, :] for a in range(4)]
            od = [OD[:, 1 + a, :] for a in range(4)]
            for ft in range(4):
                spec([Cm[:, a, ft * P:(ft + 1) * P] for a in range(4)], ev)
                spec([Sm[:, a, ft * P:(ft + 1) * P] for a in range(4)], od)
            spec([Sf[:, a, 0:1] for a in range(4)], ev, rows=1)
            spec([Cc], [EV[:, 0, :]])
            spec([Sfc], [OD[:, 0, :]])
            spec([Sfc[:, 0:1]], [EV[:, 0, :]], rows=1)

            eng.wait_ge(spec_ev, 12)
            for k in range(KT):
                if k >= 2:
                    eng.wait_ge(ut_lat, k - 1)
                    eng.wait_ge(ut_ctx, k - 1)
                for i in range(TT):
                    if k == 0:
                        eng.wait_ge(xhat_rdy, i + 1)
                    dst = B[7 if k % 2 == 0 else 0][:, 0:P] if i == 0 else B[5 + k % 2][:, (i - 1) * P:i * P]
                    last = T.transpose(dst, X[:, i, k * P:(k + 1) * P], ident)
                last.then_inc(ut_mm, 1)
            eng.wait_ge(ut_lat, KT)
            eng.wait_ge(ut_ctx, KT)

            def hyt(c):
                eng.wait_ge(hyc_rdy, c + 1)
                if c:
                    eng.wait_ge(hyt_ev, c)
                for i in range(TT):
                    a = 0 if i == 0 else 2 + P * i
                    dst = B[6][:, 0:P] if i == 0 else B[5][:, (i - 1) * P:i * P]
                    last = T.transpose(dst, HYC[c % 2][:, a:a + P], ident)
                last.then_inc(hyt_mm, 1)

            def rg_gates(c):
                for m in range(4 * c, 4 * c + 4):
                    gate, e = (m % 4) // 2, m % 2
                    if m >= 2:
                        eng.wait_ge(rg_th, m - 1)
                    w = rgw[:, 4 * gate + 2 * e + c, :]
                    mm(B[7 if m % 2 == 0 else 0][:, :], w, XC[:, c, 3 + NCTX:3 + NTOK], start=True, stop=True)
                    mm(B[5 + m % 2][:, 0:NCTX], w, XC[:, c, 0:NCTX], start=True, stop=True).then_inc(rg_mm, 1)

            for m in range(22):
                if m >= 2:
                    eng.wait_ge(proj_lat, m - 1)
                    eng.wait_ge(proj_ctx, min(m - 1, 18))
                eng.wait_ge(wh_rdy, m + 1)
                eng.wait_ge(wl_rdy, m + 1)
                wl = WL[slot_of[8 + m // 2]]
                for k in range(KT):
                    if m == 0:
                        eng.wait_ge(utl_rdy, k + 1)
                    for q, (w, u) in enumerate(((WH[m % 2][:, k, :], UTH), (WH[m % 2][:, k, :], UTL),
                                                (wl[:, k, (m % 2) * P:(m % 2 + 1) * P], UTH))):
                        first, end = k == 0 and q == 0, k == KT - 1 and q == 2
                        mm(B[1 + m % 2][:, 0:HALF], w, u[k][:, HALF:NTOK], start=first, stop=end)
                        last = mm(B[3 + m % 2][:, 0:HALF], w, u[k][:, 0:HALF], start=first, stop=end)
                last.then_inc(proj_mm, 1)
                if 2 <= m < 8:
                    hyt(m - 2)
                if m == 13:
                    eng.wait_ge(hyt_ev, 6)
                    eng.wait_ge(xc_rdy, 1)
                    eng.wait_ge(ld_attn, 16 * 4)
                    rg_gates(0)
            eng.wait_ge(proj_lat, 22)
            for i in range(TT):
                if i == 4:
                    rg_gates(1)
                    eng.wait_ge(v_ev, 1)
                for c in range(4):
                    last = T.transpose(B[1 + i % 4][:, c * P:(c + 1) * P], VC[:, c, i * P:(i + 1) * P], ident)
                last.then_inc(v_mm, 1)
            eng.wait_ge(v_ev, TT)
            for c in range(4):
                last = T.transpose(B[1][:, c * P:(c + 1) * P], KTt[:, c, 0:NCTX], ident)
            last.then_inc(nk_mm, 1)

            def mod2(p0, p1):
                for p in range(p0, p1):
                    if p >= 3:
                        eng.wait_ge(mr_ev, p - 2)
                    rows(piece(19 + p), mod2_bank(p))

            def forward(o):
                for ft in range(5):
                    if o:
                        eng.wait_ge(z_next, 5)
                    bank = B[3 + ft]
                    if ft < 4:
                        for q, mat in ((0, Cm), (1, Sf if ft == 0 else Sm)):
                            cc = 0 if q and ft == 0 else ft * P
                            for a in range(4):
                                last = mm(bank[:, q * NHY:(q + 1) * NHY], mat[:, a, cc:cc + P],
                                          HYT[:, 1 + a, 0:NHY], start=(a == 0), stop=(a == 3))
                    else:
                        mm(bank[:, 0:NHY], Cc, HYT[:, 0, 0:NHY], start=True, stop=True)
                        last = mm(bank[:, NHY:2 * NHY], Sfc, HYT[:, 0, 0:NHY], start=True, stop=True)
                    last.then_inc(z_mm, 1)

            def inverse(o):
                eng.wait_ge(y_rdy, 5 * o + 5)
                for i in (1, 2, 3, 4, 0):
                    bank = B[2 + i][:, 0:NHY] if i else B[7][:, 0:NHY]
                    if i:
                        c = (i - 1) * P
                        for ft in range(4):
                            mm(bank, Cm[:, ft, c:c + P], YA[:, ft, :], start=(ft == 0), stop=False)
                        for ft in range(4):
                            last = mm(bank, Sm[:, ft, c:c + P] if ft else Si[:, c:c + P], YB[:, ft, :],
                                      start=False, stop=(ft == 3))
                    else:
                        mm(bank, Cc, YAc, start=True, stop=False)
                        last = mm(bank, Sic, YBc, start=False, stop=True)
                    last.then_inc(inv_mm, 1)

            eng.wait_ge(rg_th, 8)
            eng.wait_ge(nk_ev, 1)
            forward(0)
            mod2(0, 5)
            inverse(0)
            mod2(5, 10)
            forward(1)
            mod2(10, 16)
            inverse(1)
            eng.wait_ge(z_next, 10)
            for c in range(2):
                for i in range(TT):
                    dst = B[5 + c][:, 0:P] if i == 0 else B[3 + c][:, (i - 1) * P:i * P]
                    last = T.transpose(dst, HYT[:, i, c * P:(c + 1) * P], ident)
                last.then_inc(hyo_mm, 1)

            def scores(u):
                h = u % 8
                r = slice(64 * (h % 2), 64 * (h % 2) + 64)
                if u >= 2:
                    eng.wait_ge(s_read, u - 1)
                if u < 8:
                    last = mm(B[u % 2][:, 0:P], QT[r, h // 2, 0:NCTX], KTt[r, h // 2, 0:NCTX], start=True, stop=True)
                else:
                    b = u // 8 - 1
                    q = QT[r, h // 2, NCTX + (3 - b) * P:NCTX + (4 - b) * P]
                    k0_ = NCTX + KEY0[b] * P
                    mm(B[u % 2][:, 0:LATW[b]], q, KTt[r, h // 2, k0_:k0_ + LATW[b]], start=True, stop=True)
                    last = mm(B[u % 2][:, LATW[b]:LATW[b] + P], q, cKT[r, h // 2, :], start=True, stop=True)
                last.then_inc(s_mm, 1)

            def ptrans(u):
                nt = 1 if u < 8 else LATW[u // 8 - 1] // P + 1
                eng.wait_ge(p_rdy, u + 1)
                if u >= 2:
                    eng.wait_ge(pt_ev, u - 1)
                for a in range(nt):
                    last = T.transpose(B[2 + u % 2][:, a * P:(a + 1) * P], PR[u % 2][:, a * P:(a + 1) * P], ident)
                last.then_inc(pt_mm, 1)

            def pv(u):
                h, blk = u % 8, u // 8
                eng.wait_ge(pt_ev, u + 1)
                if h == 0 and blk >= 2:
                    eng.wait_ge(o_rdy, blk - 1)
                if u < 8:
                    vs = [VT[:, 0, h * HD:(h + 1) * HD]]
                else:
                    b = blk - 1
                    vs = [VT[:, 1 + KEY0[b] + a, h * HD:(h + 1) * HD] for a in range(LATW[b] // P)]
                    vs.append(cV[:, h * HD:(h + 1) * HD])
                for a, v in enumerate(vs):
                    last = mm(B[4 + blk % 2][:, h * HD:(h + 1) * HD], PTs[u % 2][:, a * P:(a + 1) * P], v,
                              start=(a == 0), stop=(a == len(vs) - 1))
                last.then_inc(pv_mm, 1)

            def otrans(blk):
                eng.wait_ge(o_rdy, blk + 1)
                if blk >= 2:
                    eng.wait_ge(ot_ev, blk - 1)
                for c in range(4):
                    last = T.transpose(B[6 + blk % 2][:, c * P:(c + 1) * P], OS[blk % 2][:, c * P:(c + 1) * P], ident)
                last.then_inc(ot_mm, 1)

            eng.wait_ge(mr_ev, 16)
            eng.wait_ge(hyo_ev, 4)
            scores(0)
            for u in range(40):
                if u < 39:
                    scores(u + 1)
                ptrans(u)
                if u >= 1:
                    pv(u - 1)
                if u >= 10 and u % 8 == 2:
                    otrans(u // 8 - 1)
            pv(39)
            otrans(4)

            def u2trans(i):
                eng.wait_ge(u2_rdy, i + 1)
                for b in range(2):
                    if i:
                        eng.wait_ge(u2t_ev, 2 * i + b - 1)
                    for a in range(4):
                        last = T.transpose(B[4 + b][:, a * P:(a + 1) * P], U2[:, i, (4 * b + a) * P:(4 * b + a + 1) * P],
                                           ident)
                    last.then_inc(u2t_mm, 1)

            def logits(i):
                eng.wait_ge(u2t_ev, 2 * i + 2)
                for k in range(KT):
                    last = mm(B[6][:, 20 * i:20 * i + 20], U2T[:, k, i * P:(i + 1) * P], wrt[:, k, :],
                              start=(k == 0), stop=(k == KT - 1))
                last.then_inc(lg_mm, 1)

            eng.wait_ge(ot_ev, 5)
            eng.wait_ge(wo_in, 64)
            for i in range(TT):
                if i >= 2:
                    eng.wait_ge(mix_ev, 2 * (i - 1))
                for b in range(2):
                    for pp in range(2):
                        w = wo[2 * b + pp]
                        for k in range(KT):
                            last = mm(B[2 * (i % 2) + b][:, pp * 256:(pp + 1) * 256], MT[:, k, i * P:(i + 1) * P],
                                      w[:, k, :], start=(k == 0), stop=(k == KT - 1))
                    last.then_inc(mix_mm, 1)
                if i >= 1:
                    u2trans(i - 1)
                if i >= 2:
                    logits(i - 2)
            logits(3)
            u2trans(4)
            logits(4)
            eng.wait_ge(onehot, 1)
            for i in range(TT):
                for a in range(i + 1):
                    mm(B[7][:, NE * i:NE * (i + 1)], upper if a == i else ones, MH[:, a, :],
                       start=(a == 0), stop=(a == i))
            for a in range(TT):
                last = mm(B[7][:, NE * TT:NE * (TT + 1)], ones, MH[:, a, :], start=(a == 0), stop=(a == TT - 1))
            last.then_inc(rank_mm, 1)

            def hidden_transposed(i, j):
                done = eng.snap(i * 2 + j + 3)
                one = eng.snap(i * 2 + j + 1)
                eng.wait_ge(h_rdy, done)
                eng.wait_ge(ht_ev, one)
                for a in range(2):
                    last = T.transpose(B[6][:, a * P:(a + 1) * P], hh[j][:, 1, a * P:(a + 1) * P], ident)
                last.then_inc(ht_mm, 1)

            for s, v in ((xt_mm, 2), (gu_mm, 2), (ht_mm, 2), (dn_mm, 2)):
                eng.sem_inc(s, v)
            eng.wait_ge(mix_ev, 2 * TT)
            eng.wait_ge(slots_rdy, 2)
            np_ = eng.value_load(npair[0:1, 0:1], min_val=1, max_val=MAX_TILES // 2)
            with eng.Fori(0, np_) as i:
                for j in range(2):
                    one = eng.snap(i * 2 + j + 1)
                    rows = eng.snap(i * 16 + 16)
                    eng.wait_ge(y_evA, one)
                    eng.wait_ge(y_evB, one)
                    eng.wait_ge(xg_in[j], rows)
                    for a in range(KT):
                        last = T.transpose(B[2 * j + a // 4][:, (a % 4) * P:(a % 4 + 1) * P],
                                           xg[j][:, a * P:(a + 1) * P], ident)
                    last.then_inc(xt_mm, 1)
                for j in range(2):
                    one = eng.snap(i * 2 + j + 1)
                    win = eng.snap(i * 32 + 32)
                    eng.wait_ge(xt_evA, one)
                    eng.wait_ge(xt_evB, one)
                    eng.wait_ge(h_rdy, one)
                    eng.wait_ge(wgu_in[j], win)
                    for k in range(KT):
                        if j == 1 and k == KT - 2:
                            hidden_transposed(i, 0)
                        last = mm(B[4 + j][:, :], xgT[j][:, k, :], wgu[j][:, k, :], start=(k == 0), stop=(k == KT - 1))
                    last.then_inc(gu_mm, 1)
                for j in range(2):
                    if j == 1:
                        hidden_transposed(i, 1)
                    htd = eng.snap(i * 2 + j + 2)
                    win = eng.snap(i * 16 + 16)
                    eng.wait_ge(wdn_in[j], win)
                    eng.wait_ge(ht_ev, htd)
                    for b in range(2):
                        for k in range(2):
                            last = mm(B[2 * j + b][:, :], hT[j][:, k, :], wdn[j][:, k, b * 512:(b + 1) * 512],
                                      start=(k == 0), stop=(k == 1))
                    last.then_inc(dn_mm, 1)

        @block.vector
        def _(eng):
            count = {}

            def after(s, v=1):
                count[s] = count.get(s, 0) + v
                eng.wait_ge(s, count[s])

            def step(ins):
                ins.then_inc(dv, 1)
                after(dv)

            tt_, ts_, stt = V.tensor_tensor, V.tensor_scalar, V.scalar_tensor_tensor
            eng.wait_ge(ld_small, 16 * 8)
            eng.wait_ge(cond_rdy, 1)
            step(stt(sig, sig, 1.0, cond, ALU.add, ALU.mult))
            ts_(cond, sig, 0.5, None, ALU.mult).then_inc(modc_in, 1)
            after(modc_in)
            lam = params[:, _COLS["lam"][0]:_COLS["lam"][0] + 4]
            step(ts_(sp[:, 2, :], lam, -1.0, None, ALU.mult))
            tt_(sp[:, 1, :], sp[:, 2, :], lam, ALU.max).then_inc(sp_in, 1)
            after(sp_in)
            step(ts_(sp[:, 0, :], sp[:, 2, :], 0.0, None, ALU.max))
            eng.wait_ge(sp_exp, 1)
            step(ts_(sp[:, 2, :], sp[:, 1, :], 2.0, None, ALU.add))
            step(V.reciprocal(sp[:, 2, :], sp[:, 2, :]))
            step(tt_(sp[:, 2, :], sp[:, 1, :], sp[:, 2, :], ALU.mult))
            step(tt_(sp[:, 3, :], sp[:, 2, :], sp[:, 2, :], ALU.mult))
            step(ts_(sp[:, 4, :], sp[:, 3, :], 1.0 / 17, 1.0 / 15, ALU.mult, ALU.add))
            for q in (13, 11, 9, 7, 5, 3, 1):
                step(tt_(sp[:, 4, :], sp[:, 4, :], sp[:, 3, :], ALU.mult))
                step(ts_(sp[:, 4, :], sp[:, 4, :], 1.0 / q, None, ALU.add))
            step(tt_(sp[:, 4, :], sp[:, 4, :], sp[:, 2, :], ALU.mult))
            step(stt(sp[:, 5, :], sp[:, 4, :], 2.0, sp[:, 0, :], ALU.mult, ALU.add))
            step(ts_(sp[:, 5, :], sp[:, 5, :], -4.0, None, ALU.mult))
            step(ts_(hbias, params[:, _COLS["ba"][0]:_COLS["ba"][0] + 8], 0.5, None, ALU.mult))
            magic = 1.5 * 2.0 ** 23
            hi = 6.28125
            for layer in range(2):
                eng.wait_ge(filt_mm, layer + 1)
                bcol, fcol = col("hy_b2" if layer else "hy_b1", 0, HIDDEN), col("freq", layer, HIDDEN)
                step(ts_(FA[0:HIDDEN, NCTX:NTOK], B[2 * layer][0:HIDDEN, :], bcol, fcol, ALU.add, ALU.mult))
                step(ts_(FA[0:HIDDEN, 0:NCTX], B[2 * layer + 1][0:HIDDEN, 0:NCTX], bcol, fcol, ALU.add, ALU.mult))
                step(ts_(FB[0:HIDDEN, :], FA[0:HIDDEN, :], 1.0 / (2 * math.pi), magic, ALU.mult, ALU.add))
                step(ts_(FB[0:HIDDEN, :], FB[0:HIDDEN, :], -magic, None, ALU.add))
                step(stt(FA[0:HIDDEN, :], FB[0:HIDDEN, :], -hi, FA[0:HIDDEN, :], ALU.mult, ALU.add))
                step(stt(FA[0:HIDDEN, :], FB[0:HIDDEN, :], -(2 * math.pi - hi), FA[0:HIDDEN, :], ALU.mult, ALU.add))
                ts_(FA[0:HIDDEN, :], FA[0:HIDDEN, :], 3.1415925, -3.1415925, ALU.min, ALU.max).then_inc(filt_arg, 1)
                after(filt_arg)
            eng.wait_ge(m1_mm, 1)
            bm = params[:, 0:NMOD1].unsqueeze(2).to_broadcast([P, NMOD1, 2])
            step(tt_(modc.rearrange("p (a b) -> p a b", b=2), B[0][:, 0:32].rearrange("p (a b) -> p a b", b=2), bm, ALU.add))
            ts_(modc[:, 16:32], modc[:, 16:32], 1.0, None, ALU.add).then_inc(modc_rdy, 1)
            after(modc_rdy)
            for i in range(TT):
                eng.wait_ge(win_rdy, i + 1)
                eng.wait_ge(h3_mm, i + 1)
                b0, b1 = B[4 + 2 * (i % 2)], B[5 + 2 * (i % 2)]
                step(tt_(EV[:, i, :], b0[:, :], WN[:, 0:512], ALU.mult))
                if i < 2:
                    stt(OD[:, i, :], b1[:, :], col("not0"), WN[:, 512:1024], ALU.mult, ALU.mult).then_inc(eo_win, 1)
                    after(eo_win)
                else:
                    tt_(OD[:, i, :], b1[:, :], WN[:, 512:1024], ALU.mult).then_inc(eo_win, 1)
                    after(eo_win)
            eng.wait_ge(eo_win, TT)
            step(tt_(EV[:, :, :], EV[:, :, :], OD[:, :, :], ALU.add))
            stt(OD[:, :, :].rearrange("p a b -> p (a b)"), OD[:, :, :].rearrange("p a b -> p (a b)"), -2.0,
                EV[:, :, :].rearrange("p a b -> p (a b)"), ALU.mult, ALU.add).then_inc(eo_rdy, TT)
            after(eo_rdy, TT)

            def moments(x, i):
                step(V.bn_stats(stats[:, i, 0:6], x[:, 0:512]))
                step(V.bn_stats(stats[:, i, 6:12], x[:, 512:1024]))
                step(V.bn_aggr(mv[:, i, :], stats[:, i, :]))
                return ts_(rstd[:, i:i + 1], mv[:, i, 1:2], LN_EPS, None, ALU.add)

            def inverse_std(i):
                step(V.reciprocal(rstd[:, i:i + 1], rstd[:, i:i + 1]))
                return stt(nmr[:, i:i + 1], mv[:, i, 0:1], -1.0, rstd[:, i:i + 1], ALU.mult, ALU.mult)

            def normalise(dst, x, i, gain, bias):
                step(V.reciprocal(rstd[:, i:i + 1], rstd[:, i:i + 1]))
                step(stt(dst, x, mv[:, i, 0:1], gain, ALU.subtract, ALU.mult))
                return stt(dst, dst, rstd[:, i:i + 1], bias, ALU.mult, ALU.add)

            for i in range(TT):
                eng.wait_ge(ld_x[i], 16)
                last = moments(X[:, i, :], i)
                if i < TT - 1:
                    step(last)
            last.then_inc(var_rdy, 1)
            after(var_rdy)
            eng.wait_ge(std_rdy, 1)
            for i in range(TT):
                last = inverse_std(i)
                if i < TT - 1:
                    step(last)
            last.then_inc(xhat_in, 1)
            after(xhat_in)
            eng.wait_ge(modc_rdy, 1)

            def u_low(k):
                eng.wait_ge(uth_rdy, k + 1)
                tt_(UTL[k], UTF[:, k, :], UTH[k].bitcast(F), ALU.subtract).then_inc(utl_rdy, 1)

            for k in range(KT):
                eng.wait_ge(ut_mm, k + 1)
                ts_(UTF[:, k, 0:NCTX], B[7 if k % 2 == 0 else 0][:, 0:P], modc[:, 2 * (8 + k):2 * (8 + k) + 1],
                    modc[:, 2 * k:2 * k + 1], ALU.mult, ALU.add).then_inc(ut_ctx, 1)
                after(ut_ctx)
                if k:
                    u_low(k - 1)
            u_low(KT - 1)

            def taps(dst, src, width, wname, nk, wi, stride, bias):
                step(ts_(dst, src[:, 0:width], col(wname, wi), bias, ALU.mult, ALU.add))
                for k in range(1, nk):
                    last = stt(dst, src[:, k:k + width], col(wname, k * stride + wi), dst, ALU.mult, ALU.add)
                    if k < nk - 1:
                        step(last)
                return last

            def rg_chunk(c):
                eng.wait_ge(rg_th, 4 * c + 4)
                if c == 0:
                    pass
                step(ts_(RT[:, 0, 0, :], RT[:, 0, 0, :], 1.0, sp[:, 5, c:c + 1], ALU.add, ALU.mult))
                ts_(RT[:, 0, 1, :], RT[:, 0, 1, :], 1.0, sp[:, 5, 2 + c:3 + c], ALU.add, ALU.mult).then_inc(rg_la, 1)
                after(rg_la)
                for e in range(2):
                    step(stt(RT[:, 1, e, 0:NCTX], RT[:, 1, e, 0:NCTX], 1.0, XC[:, c, 0:NCTX], ALU.add, ALU.mult))
                    step(stt(RT[:, 1, e, NCTX:NTOK], RT[:, 1, e, NCTX:NTOK], 1.0, XC[:, c, 3 + NCTX:3 + NTOK],
                             ALU.add, ALU.mult))
                eng.wait_ge(rg_au, c + 1)
                step(ts_(RT[:, 3, :, :], RT[:, 2, :, :], 1.0, None, ALU.add))
                step(V.reciprocal(RT[:, 3, :, :], RT[:, 3, :, :]))
                tt_(RT[:, 2, :, :], RT[:, 2, :, :], RT[:, 3, :, :], ALU.mult).then_inc(rg_q, 1)
                after(rg_q)
                eng.wait_ge(rg_sq, c + 1)
                flat = lambda q: RT[:, q, :, :].rearrange("p a b -> p (a b)")
                step(stt(flat(1), flat(2), 0.5, flat(1), ALU.mult, ALU.mult))
                h0 = lambda e: col("h0", 2 * e + c)
                scan = V.tensor_tensor_scan
                step(scan(RT[:, 3, 0, 0:NCTX], RT[:, 0, 0, 0:NCTX], RT[:, 1, 0, 0:NCTX], 0.0, ALU.mult, ALU.add))
                step(scan(RT[:, 3, 0, NCTX:NTOK], RT[:, 0, 0, NCTX:NTOK], RT[:, 1, 0, NCTX:NTOK], h0(0), ALU.mult, ALU.add))
                rv = lambda q, a, b: RT[:, q, 1, a:b][:, ::-1]
                step(scan(rv(3, 0, NCTX), rv(0, 0, NCTX), rv(1, 0, NCTX), 0.0, ALU.mult, ALU.add))
                step(scan(rv(3, NCTX, NTOK), rv(0, NCTX, NTOK), rv(1, NCTX, NTOK), h0(1), ALU.mult, ALU.add))
                step(V.tensor_copy(hstate[:, c:c + 1], RT[:, 3, 0, NCTX - 1:NCTX]))
                step(V.tensor_copy(hstate[:, 2 + c:3 + c], RT[:, 3, 1, 0:1]))
                step(tt_(RT[:, 2, 0, :], RT[:, 3, 0, :], RT[:, 3, 1, :], ALU.add))
                eng.wait_ge(gel_in, 2)
                stt(XC[:, c, 0:NTOK], RT[:, 2, 0, :], 0.5, GATE[:, c, :], ALU.mult, ALU.mult).then_inc(rg_out, 1)
                after(rg_out)

            for m in range(18):
                eng.wait_ge(proj_mm, m + 1)
                src = B[3 + m % 2][:, 0:NCTX]
                lat = B[3 + m % 2][:, NCTX:HALF]
                grid = lat.rearrange("p (r c) -> p r c", r=HROWS)
                if m < 6:
                    if m < 2:
                        eng.wait_ge(pads, 1)
                    if m >= 2:
                        eng.wait_ge(hyc_rdy, m - 1)
                    step(V.tensor_copy(HYP[m % 2][:, 3 + NCTX:3 + HALF], lat))
                    V.tensor_copy(HYP[m % 2][:, 1:1 + NCTX], src).then_inc(proj_ctx, 1)
                    after(proj_ctx)
                elif m < 8:
                    if m == 6:
                        eng.wait_ge(pads, 2)
                    step(V.tensor_copy(XRP[:, m - 6, 5 + NCTX:5 + HALF], lat))
                    V.tensor_copy(XRP[:, m - 6, 2:2 + NCTX], src).then_inc(proj_ctx, 1)
                    after(proj_ctx)
                elif m < 10:
                    V.tensor_copy(GATE[:, m - 8, 0:HALF], B[3 + m % 2][:, 0:HALF]).then_inc(proj_ctx, 1)
                    after(proj_ctx)
                elif m < 14:
                    if m == 10:
                        eng.wait_ge(hyt_mm, 6)
                    view = QT[:, m - 10, NCTX:NTOK].rearrange("p (c r) -> p r c", r=ROWS)
                    step(ts_(view[:, 0:HROWS, ::-1], grid, 0.125, None, ALU.mult))
                    ts_(QT[:, m - 10, 0:NCTX], src, 0.125, None, ALU.mult).then_inc(proj_ctx, 1)
                    after(proj_ctx)
                else:
                    view = KTt[:, m - 14, NCTX:NTOK].rearrange("p (c r) -> p r c", r=ROWS)
                    step(V.tensor_copy(view[:, 0:HROWS, :], grid))
                    V.tensor_copy(KTt[:, m - 14, 0:NCTX], src).then_inc(proj_ctx, 1)
                    after(proj_ctx)
                if m < 6:
                    eng.wait_ge(proj_ctx, m + 1)
                    eng.wait_ge(proj_lat, m + 1)
                    if m >= 2:
                        eng.wait_ge(hyt_mm, m - 1)
                    taps(HYC[m % 2][:, 0:NHP - 2], HYP[m % 2], NHP - 2, "hy_cw", 3, m, 6, col("hy_cb", m)
                         ).then_inc(hyc_rdy, 1)
                    after(hyc_rdy)
                if m == 7:
                    eng.wait_ge(proj_ctx, 8)
                    eng.wait_ge(proj_lat, 8)
                    step(taps(XC[:, 0, :], XRP[:, 0, :], NXR - 3, "rg_cw", 4, 0, 2, col("rg_cb", 0)))
                    taps(XC[:, 1, :], XRP[:, 1, :], NXR - 3, "rg_cw", 4, 1, 2, col("rg_cb", 1)).then_inc(xc_rdy, 1)
                    after(xc_rdy)
            eng.wait_ge(ld_attn, 16 * 4)
            rg_chunk(0)
            rg_chunk(1)
            eng.wait_ge(rg_out, 2)
            eng.wait_ge(proj_mm, 22)
            V.tensor_copy(MT[:, 4:6, :], XC[:, :, 0:NTOK]).then_inc(rg_fin, 1)
            after(rg_fin)

            def mod2_rows(p0, p1):
                eng.wait_ge(mb_in, 16)
                for p in range(p0, p1):
                    eng.wait_ge(piece_used, 8 + p + 1)
                    dst = mrow2[:, WPC * p:WPC * (p + 1)]
                    one = 1.0 if 8 <= p < 12 else 0.0
                    stt(dst, mod2_bank(p), one, dst, ALU.add, ALU.add).then_inc(mr_ev, 1)
                    after(mr_ev)

            for o in range(2):
                for ft in range(5):
                    eng.wait_ge(z_mm, 5 * o + ft + 1)
                    ya, yb, za, zb = ycols(ft)
                    a, b = B[3 + ft][:, 0:NHY], B[3 + ft][:, NHY:2 * NHY]
                    oc = slice(o * NHY, (o + 1) * NHY)
                    if ft < 4:
                        hc, hs, hd = HC[:, ft, oc], HS[:, ft, oc], (HDm[:, oc] if ft == 0 else HC[:, ft, oc])
                    else:
                        hc, hs, hd = HCc[:, oc], HSc[:, oc], HDc[:, oc]
                    if o == 0 and ft == 0:
                        eng.wait_ge(v_mm, TT)
                    if o:
                        eng.wait_ge(z_next, 5)
                    step(tt_(ya, a, hc, ALU.mult))
                    step(tt_(za, b, hs, ALU.mult))
                    step(tt_(yb, a, hs, ALU.mult))
                    tt_(zb, b, hd, ALU.mult).then_inc(z_ev, 1)
                    after(z_ev)
                mod2_rows(10 * o, 5 + 11 * o)
                for a, i in enumerate((1, 2, 3, 4, 0)):
                    eng.wait_ge(inv_mm, 5 * o + a + 1)
                    eng.wait_ge(sk_rdy, 5 * o + 5)
                    bank = B[2 + i][:, 0:NHY] if i else B[7][:, 0:NHY]
                    step(tt_(skz(i), skz(i), bank, ALU.add))
                    tt_(HYT[:, i, 0:NHY], skz(i), HYT[:, i, (1 + o) * NHY:(2 + o) * NHY], ALU.mult).then_inc(z_next, 1)
                    after(z_next)
                if o == 0:
                    mod2_rows(5, 10)

            for u in range(40 + 2):
                if u < 40:
                    w = P if u < 8 else LATW[u // 8 - 1] + P
                    eng.wait_ge(s_mm, u + 1)
                    if u >= 2:
                        eng.wait_ge(p_rdy, u - 1)
                    if u < 8:
                        if u == 0:
                            eng.wait_ge(y_rdy, 10)
                            eng.wait_ge(mr_st, 16)
                        V.tensor_copy(TS[u % 2][:, 0:P], B[u % 2][:, 0:P]).then_inc(s_read, 1)
                        after(s_read)
                    else:
                        g = (u - 8) // 4
                        eng.wait_ge(bm_rdy, g + 1)
                        lw = w - P
                        step(tt_(TS[u % 2][:, 0:lw], B[u % 2][:, 0:lw], BM[g % 2][:, u % 4, 0:lw], ALU.add))
                        V.tensor_copy(TS[u % 2][:, lw:w], B[u % 2][:, lw:w]).then_inc(s_read, 1)
                        after(s_read)
                    eng.wait_ge(s_read, u + 1)
                    V.tensor_reduce(soft[:, 0, u:u + 1], TS[u % 2][:, 0:w], AX.X, ALU.max, negate=True).then_inc(mx_rdy, 1)
                    after(mx_rdy)
                if u >= 2 and (u - 2) % 8 == 7:
                    blk = (u - 2) // 8
                    eng.wait_ge(pv_mm, 8 * blk + 8)
                    if blk >= 2:
                        eng.wait_ge(ot_mm, blk - 1)
                    step(V.reciprocal(soft[:, 2, 8 * blk:8 * blk + 8], soft[:, 1, 8 * blk:8 * blk + 8]))
                    tt_(OS[blk % 2].rearrange("p (h d) -> p h d", h=H), B[4 + blk % 2][:, :].rearrange("p (h d) -> p h d", h=H),
                        soft[:, 2, 8 * blk:8 * blk + 8].unsqueeze(2).to_broadcast([P, H, HD]), ALU.mult).then_inc(o_rdy, 1)
                    after(o_rdy)

            for i in range(TT):
                c = 0 if i == 0 else 1
                eng.wait_ge(ld_x[i], 32)
                if i == 0:
                    eng.wait_ge(ld_g1, 32)
                for b in range(2):
                    eng.wait_ge(mix_mm, 2 * i + b + 1)
                    half = slice(512 * b, 512 * (b + 1))
                    tt_(U2[:, i, half], B[2 * (i % 2) + b][:, :], g1b[:, c, half], ALU.mult).then_inc(mix_ev, 1)
                    after(mix_ev)
                eng.wait_ge(mix_ev, 2 * i + 2)
                step(stt(X1[:, i, :], X1[:, i, :], ALPHA, U2[:, i, :], ALU.mult, ALU.add))
                moments(X1[:, i, :], i).then_inc(l1_var, 1)
                after(l1_var)
                eng.wait_ge(l1_std, i + 1)
                if i == 0:
                    eng.wait_ge(ld_late, 16 * 9)
                step(normalise(X1[:, i, :], X1[:, i, :], i, l1g, l1b))
                moments(X1[:, i, :], i).then_inc(l1b_var, 1)
                after(l1b_var)
                eng.wait_ge(l1b_std, i + 1)
                normalise(U2[:, i, :], X1[:, i, :], i, sc2b[:, c, :], sh2b[:, c, :]).then_inc(u2_rdy, 1)
                after(u2_rdy)

            iota4 = params[:, _COLS["iota4"][0]:_COLS["iota4"][0] + 4]
            i4 = iota4.unsqueeze(1).to_broadcast([P, TT, 4])

            def bc(a, m=4):
                return a.unsqueeze(2).to_broadcast([P, TT, m])

            def first_max(src, hot, mx, tmp, tmp1):
                step(V.tensor_reduce(mx, src, AX.X, ALU.max))
                step(tt_(hot, src, bc(mx), ALU.is_ge))
                step(stt(tmp, hot, -64.0, i4, ALU.mult, ALU.add))
                step(V.tensor_reduce(tmp1, tmp, AX.X, ALU.min))
                step(tt_(hot, tmp, bc(tmp1), ALU.is_equal))

            eng.wait_ge(lg_mm, TT)
            step(tt_(LO, B[6][:, 0:20 * TT].rearrange("p (a b) -> p a b", a=TT),
                      brt.unsqueeze(1).to_broadcast([P, TT, 20]), ALU.add))
            first_max(LO[:, :, 0:4], OG, GM, LT, L1)
            tt_(LG, LO[:, :, 0:4], bc(GM), ALU.subtract).then_inc(gexp_in, 1)
            after(gexp_in)
            step(tt_(E44, LO[:, :, 4:20].rearrange("p t (g j) -> p t g j", g=4),
                      OG.unsqueeze(3).to_broadcast([P, TT, 4, 4]), ALU.mult))
            step(V.tensor_reduce(ES, E44.rearrange("p t g j -> p t j g"), AX.X, ALU.add))
            first_max(ES, O1, M1, LT, L1)
            step(stt(ES, O1, -BIG, ES, ALU.mult, ALU.add))
            first_max(ES, O2, M2, LT, L1)
            tt_(DL, M2, M1, ALU.subtract).then_inc(pexp_in, 1)
            after(pexp_in)
            for o1, dst in ((O1, E1), (O2, E2)):
                step(tt_(dst, OG.unsqueeze(3).to_broadcast([P, TT, 4, 4]), o1.unsqueeze(2).to_broadcast([P, TT, 4, 4]), ALU.mult))
            tt_(MH, E1.rearrange("p t g j -> p t (g j)"), E2.rearrange("p t g j -> p t (g j)"), ALU.add).then_inc(onehot, 1)
            after(onehot)
            eng.wait_ge(gexp, 1)
            step(V.tensor_reduce(L1, LG, AX.X, ALU.add))
            step(V.reciprocal(L1, L1))
            eng.wait_ge(pexp, 1)
            step(ts_(M1, DL, 1.0, None, ALU.add))
            step(V.reciprocal(M1, M1))
            step(tt_(M1, M1, L1, ALU.mult))
            step(V.tensor_copy(wts[:, :, 0], M1))
            step(tt_(wts[:, :, 1], M1, DL, ALU.mult))
            eng.wait_ge(rank_mm, 1)
            cn = B[7][:, NE * TT:NE * (TT + 1)]
            step(ts_(TC, cn, 0.0, None, ALU.is_gt))
            for q in range(1, 5):
                step(stt(TC, cn, float(q * P), TC, ALU.is_gt, ALU.add))
            step(V.tensor_tensor_scan(TI, ones[:, 0:NE], TC, 0.0, ALU.mult, ALU.add))
            step(tt_(TC, TI, TC, ALU.subtract))
            step(ts_(TC, TC, float(P), None, ALU.mult))
            step(tt_(SL, B[7][:, 0:NE * TT].rearrange("p (a b) -> p a b", a=TT),
                      TC.unsqueeze(1).to_broadcast([P, TT, NE]), ALU.add))
            for s, e in enumerate((E1, E2)):
                step(tt_(SX, SL, e.rearrange("p t g j -> p t (g j)"), ALU.mult))
                step(V.tensor_reduce(L1, SX, AX.X, ALU.add))
                step(V.tensor_copy(slots[:, s:2 * TT:2], L1))
            i26 = params[:, _COLS["iota26"][0]:_COLS["iota26"][0] + MAX_TILES]
            step(tt_(EI, TI.unsqueeze(1).to_broadcast([P, MAX_TILES, NE]),
                      i26.unsqueeze(2).to_broadcast([P, MAX_TILES, NE]), ALU.is_le))
            step(V.tensor_reduce(EJ, EI, AX.X, ALU.add))
            step(ts_(EJ, EJ, float(NE - 1), None, ALU.min))
            V.tensor_copy(eids[:, :], EJ).then_inc(slots_rdy, 1)
            after(slots_rdy)
            e13 = params[:, _COLS["even13"][0]:_COLS["even13"][0] + 13]
            step(ts_(EJ[:, 0:13], e13, TI[:, NE - 1:NE], None, ALU.is_lt))
            step(V.tensor_reduce(L1[:, 0:1], EJ[:, 0:13], AX.X, ALU.add))
            V.tensor_copy(npair[:, :], L1[:, 0:1]).then_inc(slots_rdy, 1)
            after(slots_rdy)

            eng.sem_inc(h_rdy, 2)
            eng.sem_inc(y_evB, 2)
            eng.wait_ge(slots_rdy, 2)
            np_ = eng.value_load(npair[0:1, 0:1], min_val=1, max_val=MAX_TILES // 2)
            with eng.Fori(0, np_) as i:
                for j in range(2):
                    done = eng.snap(i * 2 + j + 3)
                    one = eng.snap(i * 2 + j + 1)
                    eng.wait_ge(xt_mm, done)
                    eng.wait_ge(gu_mm, one)
                    V.tensor_copy(xgT[j][:, 4:8, :], B[2 * j + 1][:, :].rearrange("p (a b) -> p a b", a=4)
                                  ).then_inc(xt_evB, 1)
                for j in range(2):
                    one = eng.snap(i * 2 + j + 1)
                    eng.wait_ge(th_rdy, one)
                    stt(hh[j][:, 0, :], hh[j][:, 0, :], 1.0, B[4 + j][:, 0:FE], ALU.add, ALU.mult).then_inc(hg_rdy, 1)
                    eng.wait_ge(hg_rdy, one)
                    stt(hh[j][:, 1, :], hh[j][:, 0, :], 0.5, B[4 + j][:, FE:2 * FE], ALU.mult, ALU.mult).then_inc(h_rdy, 1)
                for j in range(2):
                    done = eng.snap(i * 2 + j + 3)
                    st = eng.snap(i * 16 + 16)
                    eng.wait_ge(dn_mm, done)
                    eng.wait_ge(y_st[j], st)
                    V.tensor_copy(yy[j][:, 512:1024], B[2 * j + 1][:, :]).then_inc(y_evB, 1)

            eng.wait_ge(ld_g2, 16)
            for i in range(TT):
                c = 0 if i == 0 else 1
                eng.wait_ge(ga_w, i + 1)
                step(stt(ga[:, i, :], gb[:, i, :], wts[:, i, 1:2], ga[:, i, :], ALU.mult, ALU.add))
                step(tt_(ga[:, i, :], ga[:, i, :], g2b[:, c, :], ALU.mult))
                step(stt(X1[:, i, :], X1[:, i, :], ALPHA, ga[:, i, :], ALU.mult, ALU.add))
                moments(X1[:, i, :], i).then_inc(l2_var, 1)
                after(l2_var)
                eng.wait_ge(l2_std, i + 1)
                if i < TT - 1:
                    inverse_std(i).then_inc(l2_nmr, 1)
                    after(l2_nmr)
                else:
                    normalise(X1[:, i, :], X1[:, i, :], i, l2g, l2b).then_inc(fin_last, 1)


def dft_tables():
    def tables(L):
        k = np.arange(L)
        ang = 2.0 * np.pi * ((k[:, None] * k[None, :]) % (2 * L)) / (2 * L)
        return np.cos(ang), np.sin(ang), 1.0 - 2.0 * (k % 2)

    out = []
    c, s, alt = tables(NLAT)
    tiles = lambda m: m.reshape(4, P, -1).transpose(1, 0, 2).reshape(P, -1)
    sf = s[:, 0:P].copy()
    sf[:, 0] = alt
    si = s[0:P, :].copy()
    si[0, :] = alt
    out += [tiles(c), tiles(s), tiles(sf), si]
    c, s, alt = tables(NCTX)
    sf = s.copy()
    sf[:, 0] = alt
    si = s.copy()
    si[0, :] = alt
    out += [c, sf, si]
    return np.concatenate(out, 1).astype(np.float32)


def features():
    out = []
    for L in (NCTX, NLAT):
        pos = np.arange(L, dtype=np.float32)
        tl = np.linspace(0.0, 1.0, L, dtype=np.float32)
        bands = (FEATS - 1) // 2
        f = np.linspace(1e-4, bands - 1, bands, dtype=np.float32)
        ang = np.float32(2.0 * math.pi / L) * pos[:, None] * f[None, :]
        out.append(np.concatenate([tl[:, None], np.cos(ang), -np.sin(ang)], -1).T)
    return np.ascontiguousarray(np.concatenate(out, 1).astype(np.float32))


def window_masks():
    out = []
    for b in (0, 1, 3):
        qc = 16 * b + 15 - np.arange(P) // ROWS
        kc = 16 * KEY0[b] + np.arange(LATW[b]) // ROWS
        start = np.clip(qc - WIN_C // 2, 0, GRID - WIN_C)
        inside = (kc[None, :] >= start[:, None]) & (kc[None, :] < start[:, None] + WIN_C)
        out.append(np.where(inside, 0.0, -BIG))
    return np.concatenate(out, 1).astype(np.float32)


def kernel(**inputs):
    import concourse.bacc as bacc
    from concourse.bass_utils import run_bass_kernel_spmd

    a = {k: np.asarray(v) for k, v in inputs.items()}
    f32 = np.float32

    def cols(x):
        return x.reshape(-1, P).T

    def pad64(x):
        return np.concatenate([x.reshape(1, -1).T, np.zeros((P - HIDDEN, x.size // HIDDEN), f32)], 0)

    tn = [-np.linspace(0.0, 1.0, NCTX, dtype=f32)[:, None]]
    tn += [-np.linspace(0.0, 1.0, NLAT, dtype=f32).reshape(4, P).T]
    first = np.zeros((P, 1), f32)
    first[0, 0] = 1.0
    rep = lambda v: np.tile(np.asarray(v, f32)[None, :], (P, 1))
    parts = {
        "b_mod": cols(a["b_mod"][0, 0:P * NMOD1]), "rg_cw": cols(a["rg_conv_w"][0]), "rg_cb": cols(a["rg_conv_b"][0]),
        "ba": cols(a["rg_ba"][0]), "bx": cols(a["rg_bx"][0]), "lam": cols(a["rg_lambda"][0]),
        "h0": cols(a["state_rglru"][0, 0]), "hy_cw": cols(a["hy_conv_w"][0]), "hy_cb": cols(a["hy_conv_b"][0]),
        "hy_b1": pad64(a["hy_b1"][0]), "hy_b2": pad64(a["hy_b2"][0]),
        "freq": np.concatenate([pad64(a["hy_freq"][0, 0]), pad64(a["hy_freq"][0, 1])], 1),
        "negt": np.concatenate(tn, 1), "not0": 1 - first,
        "dc_lat": (2 - first) / (2 * NLAT), "ds_lat": 2 * (1 - first) / (2 * NLAT),
        "dc_ctx": (2 - first) / (2 * NCTX), "ds_ctx": 2 * (1 - first) / (2 * NCTX),
        "iota4": rep(np.arange(4) + 64), "iota26": rep(np.arange(MAX_TILES)), "even13": rep(2 * np.arange(13)),
    }
    params = np.concatenate([parts[n].astype(f32) for n in _COLS], 1)
    assert params.shape[1] == NPAR
    rgw = np.zeros((P, 8, P), f32)
    for g, w in enumerate((a["rg_wa"][0], a["rg_wx"][0])):
        for e in range(2):
            for n in range(4):
                o = 64 * (n % 2)
                rgw[o:o + 64, 4 * g + 2 * e + n // 2, o:o + 64] = w[e, n]
    rel = np.zeros((H, DCPAD, 2 * WIN_R - 1), f32)
    rel[:, 16:16 + 2 * WIN_C - 1, :] = a["attn_rpb"][0].transpose(0, 2, 1)
    rpb = np.stack([rel[:, :, 7 - r:15 - r] for r in range(ROWS)], 1)
    tri = np.triu(np.ones((P, P), f32), 1)
    host = {
        "b_mod2": a["b_mod"][0, P * NMOD1:],
        "x": np.concatenate([a["x_prompt"][0], a["x_sample"][0]], 0),
        "cond": np.stack([a["c_ctx"].reshape(KT, P).T, a["c"][0].reshape(KT, P).T], 2),
        "w_mod": a["w_mod"][0], "w_in": a["w_in"][0], "w_out": a["w_out"][0],
        "params": params, "ident": np.eye(P, dtype=f32), "upper": tri, "ones": np.ones((P, P), f32),
        "wrt": np.concatenate([a["router_wg"][0], a["router_we"][0]], 1).reshape(KT, P, NG + NE).transpose(1, 0, 2),
        "brt": np.concatenate([a["router_bg"][0], a["router_be"][0]]),
        "tokid": (np.arange(TT)[None, :] * P + np.arange(P)[:, None]).astype(np.int32),
        "feats": features(), "hy_w1": a["hy_w1"][0], "hy_w2": a["hy_w2"][0], "hy_w3": a["hy_w3"][0],
        "decay": a["hy_decay"][0].reshape(-1), "dft": dft_tables(),
        "cache_kT": a["cache_k"][0, 0].reshape(P, 4, P).transpose(2, 1, 0),
        "cache_v": a["cache_v"][0, 0].reshape(P, H * HD), "rgw": rgw, "skip": a["hy_skip"][0].reshape(-1),
        "masks": window_masks(), "rpb": rpb,
        "ln1_g": a["ln1_g"][0], "ln1_b": a["ln1_b"][0], "ln2_g": a["ln2_g"][0], "ln2_b": a["ln2_b"][0],
        "moe_w_gate": a["moe_w_gate"][0].reshape(NE * D, FE), "moe_w_up": a["moe_w_up"][0].reshape(NE * D, FE),
        "moe_w_down": a["moe_w_down"][0].reshape(NE * FE, D),
    }
    nc = bacc.Bacc("TRN2", target_bir_lowering=False, num_devices=1)
    arrays, t = {}, {}
    for name, v in host.items():
        v = np.ascontiguousarray(v)
        arrays["in_" + name] = v
        t[name] = nc.dram_tensor("in_" + name, v.shape, mybir.dt.from_np(v.dtype), kind="ExternalInput").ap()
    F = mybir.dt.float32
    outs = {"y": (NTOK, D), "new_k": (P, H * HD), "new_v": (P, H * HD), "new_state": (P, 4)}
    for name, shape in outs.items():
        t[name] = nc.dram_tensor("out_" + name, shape, F, kind="ExternalOutput").ap()
    for name, shape, dt in (("mod_scr", (2, P * NMOD2), F), ("u2_scr", (NTOK, D), F), ("y_scr", (MAX_TILES * P, D), F),
                            ("tok_scr", (MAX_TILES * P, 1), mybir.dt.int32)):
        t[name] = nc.dram_tensor(name, shape, dt, kind="Internal").ap()
    build(nc, t)
    r = run_bass_kernel_spmd(nc, [arrays], core_ids=[0]).results[0]
    y, k, v, s = (r["out_" + name] for name in outs)
    return (y[0:NCTX].reshape(1, NCTX, D), y[NCTX:].reshape(1, NLAT, D), k.reshape(1, 1, P, H, HD),
            v.reshape(1, 1, P, H, HD), s.T.reshape(1, 1, 2, 256))
```
